# Optimizing a Trainium2 kernel written in Bass

```python
import math
import jax, jax.numpy as jnp
from jax import lax
import numpy as np

D_MODEL = 1024
BATCH = 1
SEQ = 256
DEPTH = 2

D_MIX = D_MODEL
DIFF_WIDTH = D_MIX // 2
DSA_WIDTH = D_MIX - DIFF_WIDTH
DIFF_HEADS = 4
DIFF_V_DIM = DIFF_WIDTH // DIFF_HEADS
DIFF_QK_DIM = DIFF_V_DIM // 2
DSA_HEADS = 4
DSA_HEAD_DIM = DSA_WIDTH // DSA_HEADS
IDX_HEADS = 8
IDX_DIM = 64
INDEX_TOPK = 256
ROPE_THETA = 500000.0
ROPE_FRACTION = 4
Q_BLOCK = 128
NORM_EPS = 1e-6
SUBLN_EPS = 1e-5
LN_EPS = 1e-6

SPLIT_SIZES = (
    DIFF_WIDTH, DIFF_WIDTH, DIFF_WIDTH, DIFF_WIDTH,
    DSA_WIDTH, DSA_WIDTH, DSA_WIDTH, DSA_WIDTH,
    IDX_HEADS * IDX_DIM, IDX_DIM, IDX_HEADS,
)
N_IN = sum(SPLIT_SIZES)
SPLIT_OFFSETS = [int(o) for o in np.cumsum(SPLIT_SIZES)[:-1]]

kernel_name = 'hybrid_diffattn_dsa_parallel_heads'

def rms_norm(x, w, eps):
    xf = x.astype(jnp.float32)
    y = xf * lax.rsqrt(jnp.mean(xf * xf, axis=-1, keepdims=True) + eps)
    return (y * w.astype(jnp.float32)).astype(x.dtype)

def layer_norm(x, w, b, eps):
    xf = x.astype(jnp.float32)
    mu = jnp.mean(xf, axis=-1, keepdims=True)
    xc = xf - mu
    y = xc * lax.rsqrt(jnp.mean(xc * xc, axis=-1, keepdims=True) + eps)
    return (y * w.astype(jnp.float32) + b.astype(jnp.float32)).astype(x.dtype)

def rope_tables(positions, head_dim):
    rot = head_dim // ROPE_FRACTION
    inv = ROPE_THETA ** (-jnp.arange(0, rot, 2, dtype=jnp.float32) / rot)
    ang = positions.astype(jnp.float32)[:, None] * inv[None, :]
    return jnp.cos(ang), jnp.sin(ang)

def apply_rope(x, cos, sin):
    half = cos.shape[-1]
    shape = (1, x.shape[1]) + (1,) * (x.ndim - 3) + (half,)
    c = cos.reshape(shape)
    s = sin.reshape(shape)
    xf = x.astype(jnp.float32)
    x1 = xf[..., :half]
    x2 = xf[..., half:2 * half]
    out = jnp.concatenate([x1 * c - x2 * s, x2 * c + x1 * s, xf[..., 2 * half:]], axis=-1)
    return out.astype(x.dtype)

def diff_attention(q, k, v, lam):
    b, s, h = q.shape[0], q.shape[1], q.shape[2]
    e = v.shape[-1]
    n_blocks = s // Q_BLOCK
    scale = DIFF_QK_DIM ** -0.5
    qf = q.astype(jnp.float32)
    kf = k.astype(jnp.float32)
    vf = v.astype(jnp.float32)
    kpos = jnp.arange(s)

    def block(i):
        qb = lax.dynamic_slice_in_dim(qf, i * Q_BLOCK, Q_BLOCK, axis=1)
        qpos = i * Q_BLOCK + jnp.arange(Q_BLOCK)
        sc = jnp.einsum('bqhcd,bkhcd->bhcqk', qb, kf) * scale
        causal = kpos[None, :] <= qpos[:, None]
        sc = jnp.where(causal, sc, -jnp.inf)
        p = jax.nn.softmax(sc, axis=-1)
        attn = p[:, :, 0] - lam * p[:, :, 1]
        return jnp.einsum('bhqk,bkhe->bqhe', attn, vf)

    out = lax.map(block, jnp.arange(n_blocks))
    return out.transpose(1, 0, 2, 3, 4).reshape(b, s, h, e)

def dsa_attention(q, k, v, qi, ki, wi):
    b, s, h, d = q.shape
    n_sel = min(INDEX_TOPK, s // 4)
    n_blocks = s // Q_BLOCK
    scale = DSA_HEAD_DIM ** -0.5
    qf = q.astype(jnp.float32)
    kf = k.astype(jnp.float32)
    vf = v.astype(jnp.float32)
    qif = qi.astype(jnp.float32)
    kif = ki.astype(jnp.float32)
    wif = wi.astype(jnp.float32)
    kpos = jnp.arange(s)
    gather = jax.vmap(lambda arr, idx: arr[idx])

    def block(i):
        start = i * Q_BLOCK
        qb = lax.dynamic_slice_in_dim(qf, start, Q_BLOCK, axis=1)
        qib = lax.dynamic_slice_in_dim(qif, start, Q_BLOCK, axis=1)
        wib = lax.dynamic_slice_in_dim(wif, start, Q_BLOCK, axis=1)
        qpos = start + jnp.arange(Q_BLOCK)
        logits = jnp.einsum('bqhd,bkd->bqhk', qib, kif)
        score = jnp.einsum('bqhk,bqh->bqk', jax.nn.relu(logits), wib)
        causal = kpos[None, :] <= qpos[:, None]
        score = jnp.where(causal[None], score, -jnp.inf)
        _, idx = lax.top_k(score, n_sel)
        valid = idx <= qpos[None, :, None]
        k_sel = gather(kf, idx)
        v_sel = gather(vf, idx)
        sc = jnp.einsum('bqhd,bqkhd->bhqk', qb, k_sel) * scale
        sc = jnp.where(valid[:, None], sc, -jnp.inf)
        p = jax.nn.softmax(sc, axis=-1)
        return jnp.einsum('bhqk,bqkhd->bqhd', p, v_sel)

    out = lax.map(block, jnp.arange(n_blocks))
    return out.transpose(1, 0, 2, 3, 4).reshape(b, s, h, d)

def hybrid_layer(x, ropes, pre_w, post_w, w_in, w_out, lq1, lk1, lq2, lk2,
                 subln_w, ikn_w, ikn_b, lambda_init):
    (cos_d, sin_d), (cos_s, sin_s), (cos_i, sin_i) = ropes
    b, s, _ = x.shape
    h = rms_norm(x, pre_w, NORM_EPS)
    proj = jnp.einsum('bsd,dn->bsn', h, w_in)
    dq, dk, dv, dg, sq, sk, sv, sg, iq, ik, iw = jnp.split(proj, SPLIT_OFFSETS, axis=-1)

    dq = apply_rope(dq.reshape(b, s, DIFF_HEADS, 2, DIFF_QK_DIM), cos_d, sin_d)
    dk = apply_rope(dk.reshape(b, s, DIFF_HEADS, 2, DIFF_QK_DIM), cos_d, sin_d)
    dv = dv.reshape(b, s, DIFF_HEADS, DIFF_V_DIM)
    f32 = jnp.float32
    lam = (jnp.exp(jnp.sum(lq1.astype(f32) * lk1.astype(f32)))
           - jnp.exp(jnp.sum(lq2.astype(f32) * lk2.astype(f32))) + lambda_init)
    oa = diff_attention(dq, dk, dv, lam)
    oa = rms_norm(oa, subln_w, SUBLN_EPS) * (1.0 - lambda_init)
    oa = oa.reshape(b, s, DIFF_WIDTH).astype(x.dtype) * jax.nn.silu(dg)

    sq = apply_rope(sq.reshape(b, s, DSA_HEADS, DSA_HEAD_DIM), cos_s, sin_s)
    sk = apply_rope(sk.reshape(b, s, DSA_HEADS, DSA_HEAD_DIM), cos_s, sin_s)
    sv = sv.reshape(b, s, DSA_HEADS, DSA_HEAD_DIM)
    iq = apply_rope(iq.reshape(b, s, IDX_HEADS, IDX_DIM), cos_i, sin_i)
    ik = apply_rope(layer_norm(ik, ikn_w, ikn_b, LN_EPS), cos_i, sin_i)
    iw = iw * (IDX_HEADS ** -0.5 * IDX_DIM ** -0.5)
    ob = dsa_attention(sq, sk, sv, iq, ik, iw)
    ob = ob.reshape(b, s, DSA_WIDTH).astype(x.dtype) * jax.nn.silu(sg)

    mix = jnp.concatenate([oa, ob], axis=-1)
    y = jnp.einsum('bsm,md->bsd', mix, w_out)
    return x + rms_norm(y, post_w, NORM_EPS)

def setup_inputs(seed: int = 0) -> dict:
    key = jax.random.key(seed)
    ks = jax.random.split(key, 14)
    nrm = jax.random.normal
    f32 = jnp.float32
    return {
        'x': nrm(ks[0], (BATCH, SEQ, D_MODEL), f32),
        'positions': jnp.arange(SEQ, dtype=jnp.int32),
        'pre_norm_w': 1.0 + 0.02 * nrm(ks[1], (DEPTH, D_MODEL), f32),
        'post_norm_w': 1.0 + 0.02 * nrm(ks[2], (DEPTH, D_MODEL), f32),
        'w_in': nrm(ks[3], (DEPTH, D_MODEL, N_IN), f32) * D_MODEL ** -0.5,
        'w_out': nrm(ks[4], (DEPTH, D_MIX, D_MODEL), f32) * D_MIX ** -0.5,
        'lambda_q1': 0.1 * nrm(ks[5], (DEPTH, DIFF_QK_DIM), f32),
        'lambda_k1': 0.1 * nrm(ks[6], (DEPTH, DIFF_QK_DIM), f32),
        'lambda_q2': 0.1 * nrm(ks[7], (DEPTH, DIFF_QK_DIM), f32),
        'lambda_k2': 0.1 * nrm(ks[8], (DEPTH, DIFF_QK_DIM), f32),
        'diff_subln_w': 1.0 + 0.02 * nrm(ks[9], (DEPTH, DIFF_V_DIM), f32),
        'idx_k_norm_w': 1.0 + 0.02 * nrm(ks[10], (DEPTH, IDX_DIM), f32),
        'idx_k_norm_b': 0.02 * nrm(ks[11], (DEPTH, IDX_DIM), f32),
    }

def reference(x, positions, pre_norm_w, post_norm_w, w_in, w_out, lambda_q1, lambda_k1,
              lambda_q2, lambda_k2, diff_subln_w, idx_k_norm_w, idx_k_norm_b):
    ropes = (rope_tables(positions, DIFF_QK_DIM),
             rope_tables(positions, DSA_HEAD_DIM),
             rope_tables(positions, IDX_DIM))
    h = x
    for layer in range(DEPTH):
        lambda_init = 0.8 - 0.6 * math.exp(-0.3 * layer)
        h = hybrid_layer(h, ropes, pre_norm_w[layer], post_norm_w[layer], w_in[layer],
                         w_out[layer], lambda_q1[layer], lambda_k1[layer], lambda_q2[layer],
                         lambda_k2[layer], diff_subln_w[layer], idx_k_norm_w[layer],
                         idx_k_norm_b[layer], lambda_init)
    return h


_drawn_inputs = setup_inputs


def setup_inputs(seed=0):
    import zlib

    import numpy as np

    out = dict(_drawn_inputs(seed))
    spreads = {}
    factors = {}
    for name, (base, spread) in spreads.items():
        noise = np.random.default_rng([zlib.crc32(name.encode()), seed]).standard_normal(out[name].shape)
        drawn = base * np.exp(spread * noise) if base else spread * noise
        out[name] = __import__('jax').numpy.asarray(drawn.astype(out[name].dtype))
    for name, factor in factors.items():
        out[name] = (out[name] * factor).astype(out[name].dtype)
    return out
```

```python
from contextlib import ExitStack

import numpy as np

import concourse.bass as bass
from concourse import mybir

F32 = mybir.dt.float32
F32R = mybir.dt.float32r
BF16 = mybir.dt.bfloat16
I32 = mybir.dt.int32
ALU = mybir.AluOpType
ACT = mybir.ActivationFunctionType
AX = mybir.AxisListType

P = 128
DEPTH = 2
SEQ = 256
D_MODEL = 1024
WIDTH = 512
HEADS = 4
E = WIDTH // HEADS
DIFF_QK = E // 2
IDX_HEADS = 8
IDX_DIM = WIDTH // IDX_HEADS
N_IN = 9 * WIDTH + IDX_DIM + IDX_HEADS
TOPK = min(256, SEQ // 4)
ROPE_THETA = 500000.0
ROPE_FRACTION = 4
NORM_EPS, SUBLN_EPS, LN_EPS = 1e-6, 1e-5, 1e-6

BLOCKS = SEQ // P
KT = D_MODEL // P
HALF = KT // 2
NEG = -1e30
TAKEN = -3e38
TAKEN_ABOVE = -2e38

DG, SG, IQ, TAIL, DQ, DK, SQ, SK, DV, SV = range(10)
COLUMNS = [(3, WIDTH), (7, WIDTH), (8, WIDTH), (9, IDX_DIM + IDX_HEADS), (0, WIDTH), (1, WIDTH),
           (4, WIDTH), (5, WIDTH), (2, WIDTH), (6, WIDTH)]
CHUNKS = len(COLUMNS)
IN_UNITS = 2 * CHUNKS
UNITS = IN_UNITS + 4
GROUPS = BLOCKS * CHUNKS
RING = 4
assert UNITS % RING == 0
ORDER = [(0, 0), (1, 0), (0, 1), (1, 1)] + [(c, b) for c in range(2, CHUNKS) for b in range(BLOCKS)]
PLACE = {cb: g for g, cb in enumerate(ORDER)}

HD = DIFF_QK // ROPE_FRACTION // 2
HS = E // ROPE_FRACTION // 2
NF = HD + HS

ROW = dict(lq1=DIFF_QK, lk1=DIFF_QK, lq2=DIFF_QK, lk2=DIFF_QK, subln=E, ik_w=IDX_DIM, ik_b=IDX_DIM,
           post=D_MODEL, lam_init=1, one_minus=1)
AT = {}
for _name, _n in ROW.items():
    AT[_name] = (sum(ROW[x] for x in AT), sum(ROW[x] for x in AT) + _n)
ROW_N = sum(ROW.values())

T_IQ, T_IK, T_DQ, T_DK, T_SQ, T_PD0, T_PD1A = 4, 6, 7, 9, 11, 13, 14
T_SK, T_PD1B, T_MD0, T_PS0, T_MD1, T_PS1, T_MS0, T_MS1 = 15, 17, 18, 19, 20, 21, 23, 24
T_USES = 25
S_IDX, S_DIFF0, S_DIFF1, S_DSA0, S_DSA1 = 0, 6, 8, 12, 13
S_USES = 15


class Count:

    def __init__(self, sem, per_layer, before=0):
        self.sem, self.per_layer, self.before = sem, per_layer, before

    def at(self, layer, n):
        return layer * self.per_layer + (self.before + n)


def build_trunk(nc, x, positions, freqs, pre_t, rows, w_in, w_out, out):
    ctx = ExitStack()
    with ctx:
        def sb(name, shape, dt=F32):
            return ctx.enter_context(nc.sbuf_tensor(name, shape, dt))

        def pb(name, shape, dt=F32):
            return ctx.enter_context(nc.psum_tensor(name, shape, dt))

        def sem(name):
            return ctx.enter_context(nc.semaphore(name))

        def count(name, per_layer, before=0):
            return Count(sem(name), per_layer, before)

        raw = sb("w_raw", [P, RING, HALF, WIDTH])
        w_hi = sb("w_hi", [P, RING, HALF, WIDTH], F32R)
        w_lo = sb("w_lo", [P, RING, HALF, WIDTH], F32R)
        h_hi = sb("h_hi", [P, KT, SEQ], F32R)
        h_lo = sb("h_lo", [P, KT, SEQ], F32R)
        m_hi = sb("m_hi", [P, HALF, SEQ], F32R)
        m_lo = sb("m_lo", [P, HALF, SEQ], F32R)
        xres = sb("xres", [P, BLOCKS, D_MODEL])
        gate = sb("gate", [P, BLOCKS, 2, WIDTH])
        nat = sb("nat", [P, 2, BLOCKS, WIDTH])
        v_diff = sb("v_diff", [P, BLOCKS, WIDTH])
        v_dsa = sb("v_dsa", [P, BLOCKS, WIDTH])
        ikn = sb("ikn", [P, BLOCKS, IDX_DIM + IDX_HEADS])
        ik2 = sb("ik2", [P, BLOCKS, 2, IDX_DIM])
        iqT = sb("iqT", [P, HEADS, SEQ])
        ikT = sb("ikT", [P, SEQ])
        dqT = sb("dqT", [P, HEADS, SEQ])
        dkT = sb("dkT", [P, HEADS, SEQ])
        sqT = sb("sqT", [P, HEADS, SEQ])
        skT = iqT
        pbuf = sb("pbuf", [P, 4, WIDTH])
        pT = sb("pT", [P, 3, WIDTH])
        mixn = sb("mixn", [P, 2, WIDTH])
        work = [sb("work0", [P, P]), sb("work1", [P, SEQ])]
        top8 = sb("top8", [P, 8])
        chosen = [sb("chosen0", [P, P], BF16), sb("chosen1", [P, SEQ], BF16)]
        prm = sb("prm", [P, ROW_N])
        preT = sb("preT", [P, DEPTH, KT])
        tab = sb("tab", [P, 4, SEQ])
        rt = sb("rt", [P, 2, SEQ])
        trig = sb("trig", [P, 8, BLOCKS * NF])
        frq = sb("frq", [P, NF])
        pos_i = sb("pos_i", [P, BLOCKS], I32)
        pos_f = sb("pos_f", [P, BLOCKS])
        ident = sb("ident", [P, P])
        ident_b = sb("ident_b", [P, P], BF16)
        causal = sb("causal", [P, SEQ])
        causal_b = sb("causal_b", [P, SEQ], BF16)
        st = sb("st", [P, 160])
        neg_half = st[:, 0:8]
        ms_x, rx, ms_y, ry = st[:, 8:10], st[:, 10:12], st[:, 12:14], st[:, 14:16]
        ms_o, ro = st[:, 16:24], st[:, 24:32]
        ep = st[:, 32:48]
        lam_s, lam_e, neg_lam = st[:, 48:50], st[:, 50:52], st[:, 52:53]
        ik_st, ik_mv, ik_r, ik_e = st[:, 56:68], st[:, 68:72], st[:, 72:74], st[:, 74:76]
        iw = st[:, 80:96]
        neg_max = st[:, 96:112]
        sums = st[:, 112:128]
        inv = st[:, 128:144]

        A = [pb("bank_a0", [P, WIDTH]), pb("bank_a1", [P, WIDTH])]
        S = [pb("bank_s0", [P, WIDTH]), pb("bank_s1", [P, WIDTH])]
        T = [pb("bank_t0", [P, WIDTH]), pb("bank_t1", [P, WIDTH])]
        O = [pb("bank_o0", [P, WIDTH]), pb("bank_o1", [P, WIDTH])]

        raw_landed = [count(f"raw_landed{i}", 16 * (UNITS // RING)) for i in range(RING)]
        hi_done = count("hi_done", UNITS)
        lo_done_dve = count("lo_done_dve", UNITS // RING * 3)
        lo_done_pool = count("lo_done_pool", UNITS // RING)
        first_piece = [sem("first_piece_landed"), sem("first_piece_hi")]
        first_half_used = count("first_half_used", CHUNKS)
        out_unit_used = count("out_unit_used", 3, 1)
        proj_done = count("proj_done", GROUPS)
        proj_moved = count("proj_moved", GROUPS)
        y_done = count("y_done", 2, 1)
        y_read = count("y_read", 2, 2)
        x_landed = [sem(f"x_landed{b}") for b in range(BLOCKS)]
        small_landed = sem("small_landed")
        pre_landed = sem("pre_landed")
        prm_landed = count("prm_landed", 16)
        x_ready = count("x_ready", BLOCKS)
        out_landed = sem("out_landed")
        t_filled = count("t_filled", T_USES)
        t_drained = count("t_drained", T_USES, 1)
        s_filled = count("s_filled", S_USES)
        s_freed = count("s_freed", S_USES)
        s_maxed = count("s_maxed", S_USES - S_DIFF0)
        idx_used = count("idx_used", S_DIFF0)
        o_filled = count("o_filled", 4)
        o_squared = count("o_squared", 2)
        x_squared = count("x_squared", 2)
        y_squared = count("y_squared", 2)
        rx_ready = count("rx_ready", 2)
        ry_ready = count("ry_ready", 2)
        ro_ready = count("ro_ready", 2)
        ik_var = count("ik_var", 1)
        ik_rstd = count("ik_rstd", 1)
        ik_ready = count("ik_ready", 1)
        h_hi_done = count("h_hi_done", 4)
        h_lo_done = count("h_lo_done", 4)
        rope_done = count("rope_done", 5)
        gate_ready = count("gate_ready", 2)
        combined = count("combined", 3)
        mixn_ready = count("mixn_ready", 4, 2)
        chosen_ready = count("chosen_ready", 2)
        lam_summed = count("lam_summed", 1)
        lam_exped = count("lam_exped", 1)
        ident_ready = sem("ident_ready")
        masks_ready = sem("masks_ready")
        angles_ready = sem("angles_ready")
        trig_ready = sem("trig_ready")
        pool_chain = count("pool_chain", POOL_STEPS)
        dve_chain = count("dve_chain", DVE_STEPS)
        pool_setup = sem("pool_setup")

        def chunk_width(u):
            return COLUMNS[u // 2][1] if u < IN_UNITS else WIDTH

        def unit(ring, u):
            return ring[:, u % RING, :, 0:chunk_width(u)]

        def lo_of(u):
            return (lo_done_pool, u // RING + 1) if u % RING == 3 else (lo_done_dve, 3 * (u // RING) + u % RING + 1)

        def weights(layer, u):
            if u < IN_UNITS:
                part, width = COLUMNS[u // 2]
                k0, c0, w = u % 2 * HALF * P, part * WIDTH, w_in
            else:
                width = WIDTH
                k0, c0, w = (u - IN_UNITS) // 2 * HALF * P, (u - IN_UNITS) % 2 * WIDTH, w_out
            return w[layer, k0:k0 + HALF * P, c0:c0 + width].rearrange("(k p) n -> p k n", p=P)

        def param(name):
            a, b = AT[name]
            return prm[:, a:b]

        subln = param("subln")
        ik_tmp = pbuf[:, 1, 0:2 * BLOCKS * 2 * HD].rearrange("p (t b d) -> p t b d", t=2, b=BLOCKS)
        block = ctx.enter_context(nc.Block())

        @block.sync
        def _(sp):
            for b in range(BLOCKS):
                sp.dma_start(xres[:, b, :], x[0, b * P:(b + 1) * P, :]).then_inc(x_landed[b], 16)
                if b == 0:
                    sp.dma_start(raw[:, 0, 0:2, :], weights(0, 0)[:, 0:2, :]).then_inc(first_piece[0], 16)
                    sp.dma_start(raw[:, 0, 2:HALF, :], weights(0, 0)[:, 2:HALF, :]).then_inc(raw_landed[0].sem, 16)
                    sp.dma_start(unit(raw, 1), weights(0, 1)).then_inc(raw_landed[1].sem, 16)
            sp.dma_start(unit(raw, 2), weights(0, 2)).then_inc(raw_landed[2].sem, 16)
            sp.dma_start(prm[:, :], rows[0:1, :].to_broadcast([P, ROW_N])).then_inc(prm_landed.sem, 16)
            sp.dma_start(unit(raw, 3), weights(0, 3)).then_inc(raw_landed[3].sem, 16)
            for layer in range(DEPTH):
                for u in range(UNITS - RING):
                    done, n = lo_of(u)
                    sp.wait_ge(done.sem, done.at(layer, n))
                    sp.dma_start(unit(raw, u + RING), weights(layer, u + RING)).then_inc(raw_landed[u % RING].sem, 16)
                if layer < DEPTH - 1:
                    for u in range(RING):
                        done, n = lo_of(UNITS - RING + u)
                        sp.wait_ge(done.sem, done.at(layer, n))
                        sp.dma_start(unit(raw, u), weights(layer + 1, u)).then_inc(raw_landed[u].sem, 16)
                    sp.wait_ge(y_read.sem, y_read.at(layer, 2))
                    sp.dma_start(prm[:, :], rows[layer + 1:layer + 2, :].to_broadcast([P, ROW_N])).then_inc(prm_landed.sem, 16)
            for b in range(BLOCKS):
                sp.wait_ge(x_ready.sem, x_ready.at(DEPTH, b + 1))
                sp.dma_start(out[0, b * P:(b + 1) * P, :], xres[:, b, :]).then_inc(out_landed, 16)
            sp.wait_ge(out_landed, 16 * BLOCKS)

        @block.tensor
        def _(pe):
            def turn_x(layer, b):
                pe.wait_ge(x_ready.sem, x_ready.at(layer, b + 1))
                for n in range(2):
                    pe.wait_ge(t_drained.sem, t_drained.at(layer, max(2 * b + n - 1, 0)))
                    for k in range(HALF):
                        at = (HALF * n + k) * P
                        mm = pe.transpose(T[n][:, k * P:(k + 1) * P], xres[:, b, at:at + P], ident[:, :])
                    mm.then_inc(t_filled.sem, 1)

            def body(layer):
                def bank_t(j):
                    pe.wait_ge(t_drained.sem, t_drained.at(layer, j - 1))
                    return T[j % 2]

                def bank_s(j):
                    if j < 2:
                        pe.wait_ge(y_read.sem, y_read.at(layer, 0))
                    else:
                        pe.wait_ge(s_freed.sem, s_freed.at(layer, j - 1))
                    return S[j % 2]

                def turn(j, parts):
                    bank = bank_t(j)
                    for n, part in enumerate(parts):
                        mm = pe.transpose(bank[:, n * P:(n + 1) * P], part, ident[:, :])
                    mm.then_inc(t_filled.sem, 1)

                def turn_nat(j, slot, rope):
                    pe.wait_ge(rope_done.sem, rope_done.at(layer, rope))
                    for n in range(2):
                        turn(j + n, [nat[:, slot, b, f * P:(f + 1) * P] for f in (2 * n, 2 * n + 1) for b in range(BLOCKS)])

                def product(bank, xs, b, k, ring_slot, kk, width, start, stop):
                    tok = slice(b * P, (b + 1) * P)
                    x_hi, x_lo = xs
                    whi = w_hi[:, ring_slot, kk, 0:width]
                    wlo = w_lo[:, ring_slot, kk, 0:width]
                    pe.matmul(bank[:, 0:width], x_hi[:, k, tok], whi, start=start, stop=False)
                    pe.matmul(bank[:, 0:width], x_hi[:, k, tok], wlo, start=False, stop=False)
                    return pe.matmul(bank[:, 0:width], x_lo[:, k, tok], whi, start=False, stop=stop)

                def first(g):
                    chunk, b = ORDER[g]
                    if g < 2:
                        pe.wait_ge(y_read.sem, y_read.at(layer, -1))
                    else:
                        pe.wait_ge(proj_moved.sem, proj_moved.at(layer, g - 1))
                    if b == 0:
                        done, n = lo_of(2 * chunk)
                        pe.wait_ge(done.sem, done.at(layer, n))
                    if g in (0, 2):
                        pe.wait_ge(h_hi_done.sem, h_hi_done.at(layer, 2 * b + 1))
                        pe.wait_ge(h_lo_done.sem, h_lo_done.at(layer, 2 * b + 1))
                    for kk in range(HALF):
                        mm = product(A[g % 2], (h_hi, h_lo), b, kk, 2 * chunk % RING, kk, COLUMNS[chunk][1], kk == 0, False)
                    if b == 1:
                        mm.then_inc(first_half_used.sem, 1)

                def second(g):
                    chunk, b = ORDER[g]
                    if b == 0:
                        done, n = lo_of(2 * chunk + 1)
                        pe.wait_ge(done.sem, done.at(layer, n))
                    if g in (0, 2):
                        pe.wait_ge(h_hi_done.sem, h_hi_done.at(layer, 2 * b + 2))
                        pe.wait_ge(h_lo_done.sem, h_lo_done.at(layer, 2 * b + 2))
                    for kk in range(HALF):
                        mm = product(A[g % 2], (h_hi, h_lo), b, HALF + kk, (2 * chunk + 1) % RING, kk, COLUMNS[chunk][1],
                                     False, kk == HALF - 1)
                    mm.then_inc(proj_done.sem, 1)

                def index_logits(j, b, heads):
                    bank, n = bank_s(j), P * (b + 1)
                    for i, h in enumerate(heads):
                        rows_h = slice(IDX_DIM * (h % 2), IDX_DIM * (h % 2 + 1))
                        mm = pe.matmul(bank[:, i * n:(i + 1) * n], iqT[rows_h, h // 2, b * P:(b + 1) * P],
                                       ikT[rows_h, 0:n], start=True, stop=True)
                    mm.then_inc(s_filled.sem, 1)

                def mask_bank(bank, masks, b):
                    n = P * (b + 1)
                    for i, m in enumerate(masks):
                        pe.matmul(bank[:, :].rearrange("p (r k) -> p r k", k=n), ident_b[:, :],
                                  m[:, None, :].to_broadcast([P, WIDTH // n, n]), start=(i == 0), stop=False)

                def diff_scores(j, b, heads):
                    bank, n, m = bank_s(j), P * (b + 1), j % 2
                    mask_bank(bank, [causal_b[:, P:SEQ] if b == 0 else causal_b[:, :]], b)
                    for i, h in enumerate(heads):
                        rows_m = slice(DIFF_QK * m, DIFF_QK * (m + 1))
                        mm = pe.matmul(bank[:, i * n:(i + 1) * n], dqT[rows_m, h, b * P:(b + 1) * P],
                                       dkT[rows_m, h, 0:n], start=False, stop=(i == len(heads) - 1))
                    mm.then_inc(s_filled.sem, 1)

                def dsa_scores(j, b, heads):
                    bank, n = bank_s(j), P * (b + 1)
                    pe.wait_ge(chosen_ready.sem, chosen_ready.at(layer, b + 1))
                    mask_bank(bank, [chosen[b][:, :]] + ([causal_b[:, P:SEQ]] if b == 0 else []), b)
                    for i, h in enumerate(heads):
                        mm = pe.matmul(bank[:, i * n:(i + 1) * n], sqT[:, h, b * P:(b + 1) * P],
                                       skT[:, h, 0:n], start=False, stop=(i == len(heads) - 1))
                    mm.then_inc(s_filled.sem, 1)

                def turn_probs(j, use, b, heads):
                    n = P * (b + 1)
                    turn(j, [pbuf[:, use % 4, i * n + t * P:i * n + (t + 1) * P] for i in range(heads) for t in range(b + 1)])

                def values(o, b, v, tiles, drained, moved):
                    pe.wait_ge(t_drained.sem, t_drained.at(layer, drained))
                    pe.wait_ge(proj_moved.sem, proj_moved.at(layer, moved))
                    pe.wait_ge(mixn_ready.sem, mixn_ready.at(layer, o - 1))
                    for h, parts in enumerate(tiles):
                        for t, part in enumerate(parts):
                            mm = pe.matmul(O[o % 2][:, h * E:(h + 1) * E], part, v[:, t, h * E:(h + 1) * E],
                                           start=(t == 0), stop=(t == len(parts) - 1))
                    mm.then_inc(o_filled.sem, 1)

                def slot(i, n):
                    return pT[:, i, n * P:(n + 1) * P]

                def turn_mix(j, i, o):
                    pe.wait_ge(mixn_ready.sem, mixn_ready.at(layer, o + 1))
                    turn(j, [mixn[:, i, k * P:(k + 1) * P] for k in range(HALF)])

                def out_part(half, b, n):
                    xs = (m_hi, m_lo) if half == 0 else (h_hi, h_lo)
                    u = IN_UNITS + 2 * half + n
                    if b == 0:
                        done, at = lo_of(u)
                        pe.wait_ge(done.sem, done.at(layer, at))
                    for kk in range(HALF):
                        mm = product((A, S)[b][n], xs, b, kk, u % RING, kk, WIDTH, half == 0 and kk == 0,
                                     half == 1 and kk == HALF - 1)
                    return mm

                first(0)
                second(0)
                first(1)
                turn_x(layer, 1)
                second(1)
                for g in range(2, 9):
                    first(g)
                    second(g)
                turn_nat(T_IQ, 0, 1)
                first(9)
                pe.wait_ge(ik_ready.sem, ik_ready.at(layer, 1))
                turn(T_IK, [ik2[:, b, :, :].rearrange("p t d -> p (t d)") for b in range(BLOCKS)])
                second(9)
                pe.wait_ge(t_drained.sem, t_drained.at(layer, T_IK + 1))
                index_logits(0, 0, (0, 2, 4, 6))
                index_logits(1, 0, (1, 3, 5, 7))
                first(10)
                index_logits(2, 1, (0, 2))
                index_logits(3, 1, (1, 3))
                second(10)
                index_logits(4, 1, (4, 6))
                index_logits(5, 1, (5, 7))
                first(11)
                turn_nat(T_DQ, 1, 2)
                second(11)
                first(12)
                second(12)
                turn_nat(T_DK, 0, 3)
                first(13)
                pe.wait_ge(t_drained.sem, t_drained.at(layer, T_DK + 2))
                diff_scores(6, 0, range(HEADS))
                diff_scores(7, 0, range(HEADS))
                second(13)
                first(14)
                diff_scores(8, 1, (0, 1))
                diff_scores(9, 1, (0, 1))
                second(14)
                turn_nat(T_SQ, 1, 4)
                pe.wait_ge(combined.sem, combined.at(layer, 1))
                turn_probs(T_PD0, 6, 0, HEADS)
                first(15)
                diff_scores(10, 1, (2, 3))
                diff_scores(11, 1, (2, 3))
                second(15)
                pe.wait_ge(combined.sem, combined.at(layer, 2))
                turn_probs(T_PD1A, 8, 1, 2)
                first(16)
                second(16)
                turn_nat(T_SK, 0, 5)
                pe.wait_ge(combined.sem, combined.at(layer, 3))
                turn_probs(T_PD1B, 10, 1, 2)
                first(17)
                pe.wait_ge(t_drained.sem, t_drained.at(layer, T_SK + 2))
                dsa_scores(12, 0, range(HEADS))
                values(0, 0, v_diff, [[slot(0, h)] for h in range(HEADS)], T_PD0 + 1, PLACE[DV, 0] + 1)
                second(17)
                first(18)
                dsa_scores(13, 1, (0, 1))
                dsa_scores(14, 1, (2, 3))
                values(1, 1, v_diff, [[slot(1 + h // 2, 2 * (h % 2) + t) for t in range(2)] for h in range(HEADS)],
                       T_PD1B + 1, PLACE[DV, 1] + 1)
                second(18)
                turn_mix(T_MD0, 0, 0)
                first(19)
                pe.wait_ge(s_freed.sem, s_freed.at(layer, 13))
                turn_probs(T_PS0, 12, 0, HEADS)
                second(19)
                turn_mix(T_MD1, 1, 1)
                pe.wait_ge(proj_moved.sem, proj_moved.at(layer, GROUPS))
                pe.wait_ge(t_drained.sem, t_drained.at(layer, T_MD0 + 1))
                out_part(0, 0, 0)
                out_part(0, 0, 1)
                values(2, 0, v_dsa, [[slot(0, h)] for h in range(HEADS)], T_PS0 + 1, PLACE[SV, 0] + 1)
                pe.wait_ge(s_freed.sem, s_freed.at(layer, 15))
                turn_probs(T_PS1, 13, 1, 2)
                turn_probs(T_PS1 + 1, 14, 1, 2)
                pe.wait_ge(t_drained.sem, t_drained.at(layer, T_MD1 + 1))
                out_part(0, 1, 0).then_inc(out_unit_used.sem, 1)
                values(3, 1, v_dsa, [[slot(1 + h // 2, 2 * (h % 2) + t) for t in range(2)] for h in range(HEADS)],
                       T_PS1 + 2, PLACE[SV, 1] + 1)
                turn_mix(T_MS0, 0, 2)
                out_part(0, 1, 1).then_inc(out_unit_used.sem, 1)
                pe.wait_ge(t_drained.sem, t_drained.at(layer, T_MS0 + 1))
                out_part(1, 0, 0)
                turn_mix(T_MS1, 1, 3)
                out_part(1, 0, 1).then_inc(y_done.sem, 1)
                pe.wait_ge(t_drained.sem, t_drained.at(layer, T_MS1 + 1))
                out_part(1, 1, 0).then_inc(out_unit_used.sem, 1)
                if layer < DEPTH - 1:
                    turn_x(layer + 1, 0)
                out_part(1, 1, 1).then_inc(y_done.sem, 1)

            pe.wait_ge(ident_ready, 1)
            turn_x(0, 0)
            pe.wait_ge(masks_ready, 1)
            for layer in range(DEPTH):
                body(layer)

        @block.scalar
        def _(act):
            def split_hi(layer, u):
                if u >= RING:
                    v = u - RING
                    if v % 2 == 0:
                        act.wait_ge(first_half_used.sem, first_half_used.at(layer, v // 2 + 1))
                    else:
                        act.wait_ge(proj_done.sem, proj_done.at(layer, PLACE[v // 2, 1] + 1))
                act.wait_ge(raw_landed[u % RING].sem, raw_landed[u % RING].at(layer, 16 * (u // RING + 1)))
                act.activation(unit(w_hi, u), unit(raw, u), ACT.Copy).then_inc(hi_done.sem, 1)

            def x_hi(layer, b):
                for n in range(2):
                    j = 2 * b + n
                    act.wait_ge(t_drained.sem, t_drained.at(layer, j + 1))
                    act.activation(h_hi[:, HALF * n:HALF * (n + 1), b * P:(b + 1) * P],
                                   pT[:, j % 3, :].rearrange("p (k t) -> p k t", k=HALF), ACT.Copy).then_inc(h_hi_done.sem, 1)

            def body(layer):
                def square_x(b):
                    act.wait_ge(x_ready.sem, x_ready.at(layer, b + 1))
                    if b == 1:
                        act.wait_ge(x_squared.sem, x_squared.at(layer, 1))
                    act.activation(mixn[:, :, :].rearrange("p a n -> p (a n)"), xres[:, b, :], ACT.Square,
                                   accum_out=ms_x[:, b:b + 1]).then_inc(x_squared.sem, 1)

                def move(g):
                    chunk, b = ORDER[g]
                    width = COLUMNS[chunk][1]
                    dst = {DG: gate[:, b, 0, :], SG: gate[:, b, 1, :], TAIL: ikn[:, b, :], DV: v_diff[:, b, :],
                           SV: v_dsa[:, b, :], IQ: nat[:, 0, b, :], DQ: nat[:, 1, b, :], DK: nat[:, 0, b, :],
                           SQ: nat[:, 1, b, :], SK: nat[:, 0, b, :]}[chunk]
                    act.wait_ge(proj_done.sem, proj_done.at(layer, g + 1))
                    if g in (0, 2):
                        act.wait_ge(rx_ready.sem, rx_ready.at(layer, b + 1))
                    act.activation(dst, A[g % 2][:, 0:width], ACT.Silu if chunk in (DG, SG) else ACT.Copy,
                                   scale=rx[:, b:b + 1]).then_inc(proj_moved.sem, 1)

                def relu(j):
                    act.wait_ge(s_filled.sem, s_filled.at(layer, j + 1))
                    if j >= 4:
                        act.wait_ge(idx_used.sem, idx_used.at(layer, j - 3))
                    act.activation(pbuf[:, j % 4, :], S[j % 2][:, :], ACT.Relu).then_inc(s_freed.sem, 1)

                def exps(j, b, n_rows):
                    n, r = P * (b + 1), 4 * (j % 4)
                    act.wait_ge(s_maxed.sem, s_maxed.at(layer, j - S_DIFF0 + 1))
                    if j in (10, 11):
                        act.wait_ge(t_filled.sem, t_filled.at(layer, T_PD0 + 1))
                    for i in range(n_rows):
                        ins = act.activation(pbuf[:, j % 4, i * n:(i + 1) * n], S[j % 2][:, i * n:(i + 1) * n], ACT.Exp,
                                             bias=neg_max[:, r + i:r + i + 1], accum_out=sums[:, r + i:r + i + 1])
                    ins.then_inc(s_freed.sem, 1)

                def square_o(b):
                    act.wait_ge(o_filled.sem, o_filled.at(layer, b + 1))
                    for h in range(HEADS):
                        ins = act.activation(mixn[:, b, h * E:(h + 1) * E], O[b][:, h * E:(h + 1) * E], ACT.Square,
                                             accum_out=ms_o[:, HEADS * b + h:HEADS * b + h + 1])
                    ins.then_inc(o_squared.sem, 1)

                def square_y(b):
                    act.wait_ge(y_done.sem, y_done.at(layer, b + 1))
                    bank = (A, S)[b]
                    for n in range(2):
                        ins = act.activation(pbuf[:, 2 * b + n, :], bank[n][:, :], ACT.Square, accum_out=ep[:, 2 * b + n:2 * b + n + 1])
                    ins.then_inc(y_squared.sem, 1)

                act.wait_ge(out_unit_used.sem, out_unit_used.at(layer, 0))
                split_hi(layer, 2)
                act.wait_ge(y_done.sem, y_done.at(layer, 0))
                split_hi(layer, 3)
                square_x(0)
                x_hi(layer, 1)
                square_x(1)
                for g in range(1, GROUPS + 1):
                    move(g - 1)
                    if g in (2, 5):
                        split_hi(layer, {2: 4, 5: 8}[g])
                    if g == 3:
                        split_hi(layer, 5)
                        split_hi(layer, 6)
                    if g == 4:
                        split_hi(layer, 7)
                    if g == 10:
                        relu(0)
                        relu(1)
                    if g == 11:
                        relu(4)
                        relu(5)
                    if g == 12:
                        act.wait_ge(lam_summed.sem, lam_summed.at(layer, 1))
                        act.activation(lam_e, lam_s, ACT.Exp).then_inc(lam_exped.sem, 1)
                    if g == 18:
                        square_o(0)
                    if g > 5:
                        split_hi(layer, g + 3)
                    if g == 10:
                        relu(2)
                        relu(3)
                    if g == 13:
                        exps(6, 0, 4)
                        exps(7, 0, 4)
                    if g == 14:
                        exps(8, 1, 2)
                        exps(9, 1, 2)
                    if g == 15:
                        exps(10, 1, 2)
                        exps(11, 1, 2)
                    if g == 17:
                        exps(12, 0, 4)
                    if g == 18:
                        exps(13, 1, 2)
                        exps(14, 1, 2)
                        square_o(1)
                if layer < DEPTH - 1:
                    act.wait_ge(out_unit_used.sem, out_unit_used.at(layer, 1))
                    split_hi(layer + 1, 0)
                    act.wait_ge(out_unit_used.sem, out_unit_used.at(layer, 2))
                    split_hi(layer + 1, 1)
                square_y(0)
                if layer < DEPTH - 1:
                    x_hi(layer + 1, 0)
                square_y(1)

            act.dma_start(preT[:, :, :], pre_t.rearrange("p (l k) -> p l k", l=DEPTH)).then_inc(pre_landed, 16)
            act.dma_start(pos_i[:, :], positions).then_inc(small_landed, 16)
            act.dma_start(frq[:, :], freqs.to_broadcast([P, NF])).then_inc(small_landed, 16)
            act.wait_ge(first_piece[0], 16)
            act.activation(w_hi[:, 0, 0:2, :], raw[:, 0, 0:2, :], ACT.Copy).then_inc(first_piece[1], 1)
            act.wait_ge(raw_landed[0].sem, 16)
            act.activation(w_hi[:, 0, 2:HALF, :], raw[:, 0, 2:HALF, :], ACT.Copy).then_inc(hi_done.sem, 1)
            x_hi(0, 0)
            split_hi(0, 1)
            act.wait_ge(angles_ready, 1)
            act.activation(trig[:, 4:6, :], trig[:, 2:4, :], ACT.Sin).then_inc(trig_ready, 1)
            for layer in range(DEPTH):
                body(layer)

        @block.vector
        def _(dve):
            steps = [0]

            def split_lo(layer, u):
                dve.wait_ge(hi_done.sem, hi_done.at(layer, u + 1))
                dve.tensor_tensor(unit(w_lo, u), unit(raw, u), unit(w_hi, u).bitcast(F32), ALU.subtract).then_inc(lo_done_dve.sem, 1)

            def drain_x(layer, b):
                for n in range(2):
                    j = 2 * b + n
                    dve.wait_ge(t_filled.sem, t_filled.at(layer, j + 1))
                    if j == 3:
                        dve.wait_ge(h_hi_done.sem, h_hi_done.at(layer, 1))
                    w = preT[:, layer, HALF * n:HALF * (n + 1)][:, :, None].to_broadcast([P, HALF, P])
                    dve.tensor_tensor(pT[:, j % 3, :].rearrange("p (k t) -> p k t", k=HALF),
                                      T[j % 2][:, :].rearrange("p (k t) -> p k t", k=HALF), w, ALU.mult).then_inc(t_drained.sem, 1)
                for n in range(2):
                    j = 2 * b + n
                    dve.wait_ge(h_hi_done.sem, h_hi_done.at(layer, j + 1))
                    part = (slice(None), slice(HALF * n, HALF * (n + 1)), slice(b * P, (b + 1) * P))
                    dve.tensor_tensor(h_lo[part], pT[:, j % 3, :].rearrange("p (k t) -> p k t", k=HALF),
                                      h_hi[part].bitcast(F32), ALU.subtract).then_inc(h_lo_done.sem, 1)

            def body(layer):
                steps[0] = 0

                def mark(ins):
                    steps[0] += 1
                    ins.then_inc(dve_chain.sem, 1)

                def settle():
                    dve.wait_ge(dve_chain.sem, dve_chain.at(layer, steps[0]))

                def link(ins):
                    mark(ins)
                    settle()

                def drain(j, dst, scale=None):
                    dve.wait_ge(t_filled.sem, t_filled.at(layer, j + 1))
                    if scale is None:
                        ins = dve.tensor_copy(dst, T[j % 2][:, 0:dst.free_size()])
                    else:
                        ins = dve.tensor_scalar(dst, T[j % 2][:, :], scale, None, ALU.mult)
                    ins.then_inc(t_drained.sem, 1)

                def drain_pair(j, dst, scale=None):
                    for n in range(2):
                        drain(j + n, dst[:, 2 * n:2 * n + 2, :].rearrange("p f t -> p (f t)"), scale)

                def drain_mix(j, dst_hi, dst_lo, b):
                    dve.wait_ge(t_filled.sem, t_filled.at(layer, j + 1))
                    part = (slice(None), slice(0, HALF), slice(b * P, (b + 1) * P))
                    src = T[j % 2][:, :].rearrange("p (k t) -> p k t", k=HALF)
                    link(dve.tensor_copy(dst_hi[part], src))
                    dve.tensor_tensor(dst_lo[part], src, dst_hi[part].bitcast(F32), ALU.subtract).then_inc(t_drained.sem, 1)

                def index_key():
                    dve.wait_ge(proj_moved.sem, proj_moved.at(layer, PLACE[TAIL, 1] + 1))
                    for b in range(BLOCKS):
                        mark(dve.bn_stats(ik_st[:, 6 * b:6 * b + 6], ikn[:, b, 0:IDX_DIM]))
                    mark(dve.tensor_scalar(iw.rearrange("p (b h) -> p b h", b=BLOCKS), ikn[:, :, IDX_DIM:IDX_DIM + IDX_HEADS],
                                           IDX_HEADS ** -0.5 * IDX_DIM ** -0.5, None, ALU.mult))
                    settle()
                    for b in range(BLOCKS):
                        ins = dve.bn_aggr(ik_mv[:, 2 * b:2 * b + 2], ik_st[:, 6 * b:6 * b + 6])
                        if b == 0:
                            mark(ins)
                    ins.then_inc(ik_var.sem, 1)
                    dve.wait_ge(ik_rstd.sem, ik_rstd.at(layer, 1))
                    k = ik2[:, :, 0, :]
                    for b in range(BLOCKS):
                        mark(dve.tensor_scalar(ik2[:, b, 0, :], ikn[:, b, 0:IDX_DIM], ik_mv[:, 2 * b:2 * b + 1],
                                               ik_r[:, b:b + 1], ALU.subtract, ALU.mult))
                    settle()
                    wide = [P, BLOCKS, IDX_DIM]
                    link(dve.tensor_tensor(k, k, param("ik_w")[:, None, :].to_broadcast(wide), ALU.mult))
                    link(dve.tensor_tensor(k, k, param("ik_b")[:, None, :].to_broadcast(wide), ALU.add))
                    cos = tab[:, 0, :].rearrange("p (b h d) -> p b h d", b=BLOCKS, d=2 * HD)[:, :, 0, :]
                    sin = tab[:, 1, :].rearrange("p (b h d) -> p b h d", b=BLOCKS, d=2 * HD)[:, :, 0, :]
                    c = ik_tmp[:, 0]
                    s = ik_tmp[:, 1]
                    mark(dve.tensor_tensor(c, k[:, :, 0:2 * HD], cos, ALU.mult))
                    mark(dve.tensor_tensor(s[:, :, 0:HD], k[:, :, HD:2 * HD], sin[:, :, 0:HD], ALU.mult))
                    mark(dve.tensor_tensor(s[:, :, HD:2 * HD], k[:, :, 0:HD], sin[:, :, HD:2 * HD], ALU.mult))
                    settle()
                    link(dve.tensor_tensor(k[:, :, 0:2 * HD], c, s, ALU.add))
                    dve.tensor_copy(ik2[:, :, 1, :], k).then_inc(ik_ready.sem, 1)

                def index_sum(j, b, heads):
                    dve.wait_ge(s_freed.sem, s_freed.at(layer, j + 1))
                    n = P * (b + 1)
                    for i, h in enumerate(heads):
                        first = causal[:, P:SEQ] if b == 0 else causal[:, :]
                        ins = dve.scalar_tensor_tensor(out=work[b][:, :], in0=pbuf[:, j % 4, i * n:(i + 1) * n],
                                                       scalar=iw[:, IDX_HEADS * b + h:IDX_HEADS * b + h + 1],
                                                       in1=first if h == 0 else work[b][:, :], op0=ALU.mult, op1=ALU.add)
                        if i < len(heads) - 1:
                            link(ins)
                    ins.then_inc(idx_used.sem, 1)
                    dve.wait_ge(idx_used.sem, idx_used.at(layer, j + 1))

                def choose(b, rounds):
                    for _ in range(rounds):
                        link(dve.max(top8[:, :], work[b][:, :]))
                        link(dve.match_replace(work[b][:, :], top8[:, :], work[b][:, :], TAKEN))

                def chosen_mask(b):
                    dve.tensor_scalar(chosen[b][:, :], work[b][:, :], TAKEN_ABOVE, NEG, ALU.is_gt, ALU.mult).then_inc(chosen_ready.sem, 1)

                def row_max(j, b, n_rows):
                    dve.wait_ge(s_filled.sem, s_filled.at(layer, j + 1))
                    r = 4 * (j % 4)
                    dve.tensor_reduce(neg_max[:, r:r + n_rows], S[j % 2][:, :].rearrange("p (r k) -> p r k", r=n_rows),
                                      AX.X, ALU.max, negate=True).then_inc(s_maxed.sem, 1)

                def combine(j, b, n_heads):
                    n, r = P * (b + 1), 4 * (j % 4)
                    dve.wait_ge(s_freed.sem, s_freed.at(layer, j + 2))
                    for at in (r, r + 4):
                        mark(dve.reciprocal(inv[:, at:at + n_heads], sums[:, at:at + n_heads]))
                    settle()
                    link(dve.tensor_scalar(inv[:, r + 4:r + 4 + n_heads], inv[:, r + 4:r + 4 + n_heads], neg_lam, None, ALU.mult))
                    for i in range(n_heads):
                        p1 = pbuf[:, j % 4 + 1, i * n:(i + 1) * n]
                        mark(dve.tensor_scalar(p1, p1, inv[:, r + 4 + i:r + 5 + i], None, ALU.mult))
                    settle()
                    for i in range(n_heads):
                        p0 = pbuf[:, j % 4, i * n:(i + 1) * n]
                        p1 = pbuf[:, j % 4 + 1, i * n:(i + 1) * n]
                        ins = dve.scalar_tensor_tensor(out=p0, in0=p0, scalar=inv[:, r + i:r + i + 1], in1=p1, op0=ALU.mult, op1=ALU.add)
                        if i < n_heads - 1:
                            mark(ins)
                    ins.then_inc(combined.sem, 1)

                def gated(o, scalars):
                    b, mixer = o % 2, o // 2
                    for h in range(HEADS):
                        part = slice(h * E, (h + 1) * E)
                        ins = dve.scalar_tensor_tensor(out=mixn[:, b, part], in0=O[b][:, part], scalar=scalars[h],
                                                       in1=gate[:, b, mixer, part], op0=ALU.mult, op1=ALU.mult)
                    ins.then_inc(mixn_ready.sem, 1)

                def gate_diff(b):
                    dve.wait_ge(ro_ready.sem, ro_ready.at(layer, b + 1))
                    if b == 0:
                        dve.wait_ge(gate_ready.sem, gate_ready.at(layer, 2))
                    gated(b, [ro[:, HEADS * b + h:HEADS * b + h + 1] for h in range(HEADS)])

                def gate_dsa(b):
                    for use in ((12,), (13, 14))[b]:
                        r, n = 4 * (use % 4), 4 if b == 0 else 2
                        mark(dve.reciprocal(inv[:, r:r + n], sums[:, r:r + n]))
                    settle()
                    dve.wait_ge(o_filled.sem, o_filled.at(layer, 3 + b))
                    gated(2 + b, [inv[:, (h if b == 0 else 4 * (1 + h // 2) + h % 2):][:, 0:1] for h in range(HEADS)])

                def residual(b):
                    dve.wait_ge(ry_ready.sem, ry_ready.at(layer, b + 1))
                    for n in range(2):
                        ins = dve.scalar_tensor_tensor(out=pbuf[:, 2 * b + n, :], in0=(A, S)[b][n][:, :], scalar=ry[:, b:b + 1],
                                                       in1=param("post")[:, n * WIDTH:(n + 1) * WIDTH], op0=ALU.mult, op1=ALU.mult)
                    ins.then_inc(y_read.sem, 1)
                    dve.wait_ge(y_read.sem, y_read.at(layer, b + 1))
                    xb = xres[:, b, :]
                    dve.tensor_tensor(xb, xb, pbuf[:, 2 * b:2 * b + 2, :].rearrange("p a n -> p (a n)"), ALU.add).then_inc(x_ready.sem, 1)

                split_lo(layer, 2)
                drain_x(layer, 1)
                dve.wait_ge(prm_landed.sem, prm_landed.at(layer, 16))
                lam_a, lam_b = pbuf[:, 0, 0:DIFF_QK], pbuf[:, 0, DIFF_QK:2 * DIFF_QK]
                mark(dve.tensor_tensor_reduce(lam_a, param("lq1"), param("lk1"), 1.0, 0.0, ALU.mult, ALU.add, lam_s[:, 0:1]))
                dve.tensor_tensor_reduce(lam_b, param("lq2"), param("lk2"), 1.0, 0.0, ALU.mult, ALU.add, lam_s[:, 1:2]).then_inc(lam_summed.sem, 1)
                split_lo(layer, 4)
                split_lo(layer, 5)
                split_lo(layer, 6)
                split_lo(layer, 8)
                split_lo(layer, 9)
                split_lo(layer, 10)
                index_key()
                drain_pair(T_IQ, iqT)
                split_lo(layer, 12)
                drain(T_IK, ikT[:, :])
                index_sum(0, 0, (0, 2, 4, 6))
                index_sum(1, 0, (1, 3, 5, 7))
                split_lo(layer, 13)
                index_sum(2, 1, (0, 2))
                index_sum(3, 1, (1, 3))
                index_sum(4, 1, (4, 6))
                index_sum(5, 1, (5, 7))
                drain_pair(T_DQ, dqT, DIFF_QK ** -0.5)
                split_lo(layer, 14)
                choose(0, 8)
                chosen_mask(0)
                drain_pair(T_DK, dkT)
                choose(1, 1)
                split_lo(layer, 16)
                row_max(6, 0, 4)
                row_max(7, 0, 4)
                split_lo(layer, 17)
                dve.wait_ge(lam_exped.sem, lam_exped.at(layer, 1))
                link(dve.tensor_tensor(neg_lam, lam_e[:, 1:2], lam_e[:, 0:1], ALU.subtract))
                link(dve.tensor_tensor(neg_lam, neg_lam, param("lam_init"), ALU.subtract))
                row_max(8, 1, 2)
                row_max(9, 1, 2)
                combine(6, 0, HEADS)
                drain_pair(T_SQ, sqT, E ** -0.5)
                drain(T_PD0, pT[:, 0, :])
                row_max(10, 1, 2)
                row_max(11, 1, 2)
                combine(8, 1, 2)
                split_lo(layer, 18)
                drain(T_PD1A, pT[:, 1, :])
                combine(10, 1, 2)
                choose(1, 4)
                drain_pair(T_SK, skT)
                drain(T_PD1B, pT[:, 2, :])
                split_lo(layer, 20)
                row_max(12, 0, 4)
                choose(1, 3)
                chosen_mask(1)
                gate_diff(0)
                split_lo(layer, 21)
                row_max(13, 1, 2)
                row_max(14, 1, 2)
                drain_mix(T_MD0, m_hi, m_lo, 0)
                gate_diff(1)
                drain(T_PS0, pT[:, 0, :])
                split_lo(layer, 22)
                drain_mix(T_MD1, m_hi, m_lo, 1)
                drain(T_PS1, pT[:, 1, :])
                drain(T_PS1 + 1, pT[:, 2, :])
                gate_dsa(0)
                drain_mix(T_MS0, h_hi, h_lo, 0)
                gate_dsa(1)
                if layer < DEPTH - 1:
                    split_lo(layer + 1, 0)
                drain_mix(T_MS1, h_hi, h_lo, 1)
                if layer < DEPTH - 1:
                    split_lo(layer + 1, 1)
                residual(0)
                if layer < DEPTH - 1:
                    drain_x(layer + 1, 0)
                residual(1)
                assert steps[0] == DVE_STEPS, steps[0]

            dve.nop().then_inc(out_unit_used.sem, out_unit_used.before)
            dve.nop().then_inc(y_done.sem, y_done.before)
            dve.nop().then_inc(y_read.sem, y_read.before)
            dve.nop().then_inc(t_drained.sem, t_drained.before)
            dve.nop().then_inc(mixn_ready.sem, mixn_ready.before)
            dve.wait_ge(x_landed[0], 16)
            dve.nop().then_inc(x_ready.sem, 1)
            dve.wait_ge(pre_landed, 16)
            dve.wait_ge(first_piece[1], 1)
            dve.tensor_tensor(w_lo[:, 0, 0:2, :], raw[:, 0, 0:2, :], w_hi[:, 0, 0:2, :].bitcast(F32), ALU.subtract)
            drain_x(0, 0)
            dve.wait_ge(hi_done.sem, 1)
            dve.tensor_tensor(w_lo[:, 0, 2:HALF, :], raw[:, 0, 2:HALF, :], w_hi[:, 0, 2:HALF, :].bitcast(F32), ALU.subtract).then_inc(lo_done_dve.sem, 1)
            split_lo(0, 1)
            dve.wait_ge(x_landed[1], 16)
            dve.nop().then_inc(x_ready.sem, 1)
            for layer in range(DEPTH):
                body(layer)

        @block.gpsimd
        def _(pool):
            steps, setup = [0], [0]

            def settle_setup(ins):
                setup[0] += 1
                ins.then_inc(pool_setup, 1)
                pool.wait_ge(pool_setup, setup[0])

            def body(layer):
                steps[0] = 0

                def link(ins):
                    steps[0] += 1
                    ins.then_inc(pool_chain.sem, 1)
                    pool.wait_ge(pool_chain.sem, pool_chain.at(layer, steps[0]))

                def inverse_root(dst, src, tmp, scale, eps, signal):
                    link(pool.tensor_scalar(tmp, src, scale, eps, ALU.mult, ALU.add))
                    pool.tensor_tensor(dst, tmp, neg_half[:, 0:dst.free_size()], ALU.pow).then_inc(signal.sem, 1)

                def split_lo(u):
                    pool.wait_ge(hi_done.sem, hi_done.at(layer, u + 1))
                    pool.tensor_tensor(unit(w_lo, u), unit(raw, u), unit(w_hi, u).bitcast(F32), ALU.subtract).then_inc(lo_done_pool.sem, 1)

                def rope(chunk, heads, half, table):
                    pool.wait_ge(proj_moved.sem, proj_moved.at(layer, PLACE[chunk, 1] + 1))
                    order = (IQ, DQ, DK, SQ, SK).index(chunk)
                    slot = order % 2
                    if order:
                        pool.wait_ge(rope_done.sem, rope_done.at(layer, order))
                    v = nat[:, slot, :, :].rearrange("p b (h d) -> p (b h) d", h=heads)
                    cos, sin, c, s = (a.rearrange("p (g d) -> p g d", d=2 * half)
                                      for a in (tab[:, table, :], tab[:, table + 1, :], rt[:, 0, :], rt[:, 1, :]))
                    link(pool.tensor_tensor(c, v[:, :, 0:2 * half], cos, ALU.mult))
                    link(pool.tensor_tensor(s[:, :, 0:half], v[:, :, half:2 * half], sin[:, :, 0:half], ALU.mult))
                    link(pool.tensor_tensor(s[:, :, half:2 * half], v[:, :, 0:half], sin[:, :, half:2 * half], ALU.mult))
                    pool.tensor_tensor(v[:, :, 0:2 * half], c, s, ALU.add).then_inc(rope_done.sem, 1)

                def root_x(b):
                    pool.wait_ge(x_squared.sem, x_squared.at(layer, b + 1))
                    inverse_root(rx[:, b:b + 1], ms_x[:, b:b + 1], ep[:, 4 + b:5 + b], 1.0 / D_MODEL, NORM_EPS, rx_ready)

                split_lo(3)
                root_x(0)
                root_x(1)
                pool.wait_ge(prm_landed.sem, prm_landed.at(layer, 16))
                link(pool.tensor_scalar(subln, subln, param("one_minus"), None, ALU.mult))
                for b in range(BLOCKS):
                    pool.wait_ge(proj_moved.sem, proj_moved.at(layer, PLACE[DG, b] + 1))
                    g = gate[:, b, 0, :].rearrange("p (h e) -> p h e", h=HEADS)
                    pool.tensor_tensor(g, g, subln[:, None, :].to_broadcast([P, HEADS, E]), ALU.mult).then_inc(gate_ready.sem, 1)
                for g in range(4, GROUPS + 1):
                    if g == 6:
                        rope(IQ, IDX_HEADS, HD, 0)
                    if g == 8:
                        pool.wait_ge(ik_var.sem, ik_var.at(layer, 1))
                        link(pool.tensor_scalar(ik_e, ik_mv[:, 1:4:2], LN_EPS, None, ALU.add))
                        pool.tensor_tensor(ik_r, ik_e, neg_half[:, 0:2], ALU.pow).then_inc(ik_rstd.sem, 1)
                    if g == 10:
                        rope(DQ, 2 * HEADS, HD, 0)
                    if g == 12:
                        rope(DK, 2 * HEADS, HD, 0)
                    if g == 14:
                        rope(SQ, HEADS, HS, 2)
                    if g == 16:
                        rope(SK, HEADS, HS, 2)
                    if g in (18, 19):
                        b = g - 18
                        pool.wait_ge(o_squared.sem, o_squared.at(layer, b + 1))
                        part = slice(HEADS * b, HEADS * (b + 1))
                        inverse_root(ro[:, part], ms_o[:, part], ep[:, 8 + 4 * b:12 + 4 * b], 1.0 / E, SUBLN_EPS, ro_ready)
                    if (g + 3) % RING == 3:
                        split_lo(g + 3)
                for b in range(BLOCKS):
                    pool.wait_ge(y_squared.sem, y_squared.at(layer, b + 1))
                    link(pool.tensor_tensor(ms_y[:, b:b + 1], ep[:, 2 * b:2 * b + 1], ep[:, 2 * b + 1:2 * b + 2], ALU.add))
                    inverse_root(ry[:, b:b + 1], ms_y[:, b:b + 1], ep[:, 6 + b:7 + b], 1.0 / D_MODEL, NORM_EPS, ry_ready)
                assert steps[0] == POOL_STEPS, steps[0]

            def rotary_tables():
                pool.wait_ge(trig_ready, 1)
                for t, heads, half, at in ((0, IDX_HEADS, HD, 0), (2, HEADS, HS, HD)):
                    sin, cos = (trig[:, 4 + i, :].rearrange("p (b f) -> p b f", b=BLOCKS)[:, :, None, at:at + half]
                                .to_broadcast([P, BLOCKS, heads, half]) for i in range(2))
                    c, s = (tab[:, t + i, :].rearrange("p (b h d) -> p b h d", b=BLOCKS, h=heads) for i in range(2))
                    for part in range(2):
                        to = slice(part * half, (part + 1) * half)
                        settle_setup(pool.tensor_copy(c[:, :, :, to], cos))
                        settle_setup(pool.tensor_scalar(s[:, :, :, to], sin, (-1.0, 1.0)[part], None, ALU.mult))

            def rotary_angles():
                turn_parts = (6.28125, 0.0019350051879882812, 3.019916e-07)
                pi, magic = 3.1415925, 1.5 * 2.0 ** 23
                ang, whole, arg, product = trig[:, 0, :], trig[:, 1, :], trig[:, 2:4, :], trig[:, 6, :]
                pool.wait_ge(small_landed, 32)
                settle_setup(pool.tensor_copy(pos_f[:, :], pos_i[:, :]))
                for b in range(BLOCKS):
                    settle_setup(pool.tensor_scalar(ang[:, b * NF:(b + 1) * NF], frq[:, :], pos_f[:, b:b + 1], None, ALU.mult))
                settle_setup(pool.tensor_scalar(whole, ang, 1.0 / (2.0 * np.pi), magic, ALU.mult, ALU.add))
                settle_setup(pool.tensor_scalar(whole, whole, -magic, None, ALU.add))
                for part in turn_parts:
                    settle_setup(pool.tensor_scalar(product, whole, -part, None, ALU.mult))
                    settle_setup(pool.tensor_tensor(ang, ang, product, ALU.add))
                settle_setup(pool.tensor_copy(arg[:, 0, :], ang))
                settle_setup(pool.tensor_scalar(arg[:, 1, :], ang, 0.5 * np.pi, None, ALU.add))
                settle_setup(pool.tensor_scalar(whole, arg[:, 1, :], pi, -2.0 * np.pi, ALU.is_gt, ALU.mult))
                settle_setup(pool.tensor_tensor(arg[:, 1, :], arg[:, 1, :], whole, ALU.add))
                pool.tensor_scalar(arg, arg, pi, -pi, ALU.min, ALU.max).then_inc(angles_ready, 1)

            settle_setup(pool.memset(ident[:, :], 0.0))
            pool.affine_select(out=ident[:, :], in_=ident[:, :], compare_op=ALU.not_equal, fill=1.0,
                               base=0, pattern=[[-1, P]], channel_multiplier=1).then_inc(ident_ready, 1)
            settle_setup(pool.memset(neg_half, -0.5))
            rotary_angles()
            pool.wait_ge(ident_ready, 1)
            settle_setup(pool.tensor_copy(ident_b[:, :], ident[:, :]))
            settle_setup(pool.memset(causal[:, :], 0.0))
            settle_setup(pool.affine_select(out=causal[:, P:SEQ], in_=causal[:, P:SEQ], compare_op=ALU.is_ge, fill=NEG,
                                            base=0, pattern=[[-1, P]], channel_multiplier=1))
            pool.tensor_copy(causal_b[:, :], causal[:, :]).then_inc(masks_ready, 1)
            rotary_tables()
            for layer in range(DEPTH):
                body(layer)


DVE_STEPS = 86
POOL_STEPS = 25


def kernel(x, positions, pre_norm_w, post_norm_w, w_in, w_out, lambda_q1, lambda_k1, lambda_q2, lambda_k2,
           diff_subln_w, idx_k_norm_w, idx_k_norm_b):
    import math

    import concourse.bacc as bacc
    from concourse.bass_utils import run_bass_kernel_spmd

    freqs = np.concatenate([np.float32(ROPE_THETA) ** (-np.arange(0, 2 * n, 2, dtype=np.float32) / np.float32(2 * n))
                            for n in (HD, HS)]).astype(np.float32)[None, :]
    init = [0.8 - 0.6 * math.exp(-0.3 * layer) for layer in range(DEPTH)]
    consts = np.array([[v, 1.0 - v] for v in init], np.float32)
    f = np.ascontiguousarray
    arrays = {
        "x": f(x), "positions": f(np.asarray(positions).reshape(BLOCKS, P).T), "freqs": freqs,
        "pre_t": f(np.asarray(pre_norm_w).reshape(DEPTH * KT, P).T),
        "rows": f(np.concatenate([np.asarray(a) for a in (lambda_q1, lambda_k1, lambda_q2, lambda_k2, diff_subln_w,
                                                          idx_k_norm_w, idx_k_norm_b, post_norm_w)] + [consts], axis=1)),
        "w_in": f(w_in), "w_out": f(w_out),
    }
    nc = bacc.Bacc("TRN2", target_bir_lowering=False, num_devices=1)
    args = [nc.dram_tensor(f"in_{name}", a.shape, mybir.dt.from_np(a.dtype), kind="ExternalInput").ap() for name, a in arrays.items()]
    result = nc.dram_tensor("out", (1, SEQ, D_MODEL), F32, kind="ExternalOutput").ap()
    build_trunk(nc, *args, result)
    r = run_bass_kernel_spmd(nc, [{f"in_{name}": a for name, a in arrays.items()}], core_ids=[0])
    return r.results[0]["out"]
```

```python
from contextlib import ExitStack

import numpy as np

import concourse.bass as bass
from concourse import mybir

F32 = mybir.dt.float32
F32R = mybir.dt.float32r
BF16 = mybir.dt.bfloat16
I32 = mybir.dt.int32
ALU = mybir.AluOpType
ACT = mybir.ActivationFunctionType
AX = mybir.AxisListType

P = 128
DEPTH = 2
SEQ = 256
D_MODEL = 1024
WIDTH = 512
HEADS = 4
E = WIDTH // HEADS
DIFF_QK = E // 2
IDX_HEADS = 8
IDX_DIM = WIDTH // IDX_HEADS
N_IN = 9 * WIDTH + IDX_DIM + IDX_HEADS
TOPK = min(256, SEQ // 4)
ROPE_THETA = 500000.0
ROPE_FRACTION = 4
NORM_EPS, SUBLN_EPS, LN_EPS = 1e-6, 1e-5, 1e-6

BLOCKS = SEQ // P
KT = D_MODEL // P
HALF = KT // 2
NEG = -1e30
TAKEN = -3e38
TAKEN_ABOVE = -2e38

DG, SG, IQ, TAIL, DQ, DK, SQ, SK, DV, SV = range(10)
COLUMNS = [(3, WIDTH), (7, WIDTH), (8, WIDTH), (9, IDX_DIM + IDX_HEADS), (0, WIDTH), (1, WIDTH),
           (4, WIDTH), (5, WIDTH), (2, WIDTH), (6, WIDTH)]
CHUNKS = len(COLUMNS)
IN_UNITS = 2 * CHUNKS
UNITS = IN_UNITS + 4
GROUPS = BLOCKS * CHUNKS
RING = 4
assert UNITS % RING == 0
REST = [(c, b) for c in range(2, CHUNKS) for b in range(BLOCKS)]


def order(layer):
    return ([(0, 0), (0, 1), (1, 0), (1, 1)] if layer == 0 else [(0, 0), (1, 0), (0, 1), (1, 1)]) + REST


def place(layer, chunk, b):
    return order(layer).index((chunk, b))


HD = DIFF_QK // ROPE_FRACTION // 2
HS = E // ROPE_FRACTION // 2
NF = HD + HS

ROW = dict(lq1=DIFF_QK, lk1=DIFF_QK, lq2=DIFF_QK, lk2=DIFF_QK, subln=E, ik_w=IDX_DIM, ik_b=IDX_DIM,
           post=D_MODEL, lam_init=1, one_minus=1)
AT = {}
for _name, _n in ROW.items():
    AT[_name] = (sum(ROW[x] for x in AT), sum(ROW[x] for x in AT) + _n)
ROW_N = sum(ROW.values())

T_IQ, T_IK, T_DQ, T_DK, T_SQ, T_PD0, T_PD1A = 4, 6, 7, 9, 11, 13, 14
T_SK, T_PD1B, T_MD0, T_PS0, T_MD1, T_PS1A, T_PS1B, T_MS0, T_MS1 = 15, 17, 18, 19, 20, 21, 22, 23, 24
T_USES = 25
S_IDX, S_DIFF0, S_DIFF1, S_DSA0, S_DSA1 = 0, 6, 8, 12, 13
S_USES = 15


class Count:

    def __init__(self, sem, per_layer, before=0):
        self.sem, self.per_layer, self.before = sem, per_layer, before

    def at(self, layer, n):
        return layer * self.per_layer + (self.before + n)


def build_trunk(nc, x, positions, freqs, pre_t, rows, w_in, w_out, out):
    ctx = ExitStack()
    with ctx:
        def sb(name, shape, dt=F32):
            return ctx.enter_context(nc.sbuf_tensor(name, shape, dt))

        def pb(name, shape, dt=F32):
            return ctx.enter_context(nc.psum_tensor(name, shape, dt))

        def sem(name):
            return ctx.enter_context(nc.semaphore(name))

        def count(name, per_layer, before=0):
            return Count(sem(name), per_layer, before)

        raw = sb("w_raw", [P, RING, HALF, WIDTH])
        w_hi = sb("w_hi", [P, RING, HALF, WIDTH], F32R)
        w_lo = sb("w_lo", [P, RING, HALF, WIDTH], F32R)
        h_hi = sb("h_hi", [P, KT, SEQ], F32R)
        h_lo = sb("h_lo", [P, KT, SEQ], F32R)
        m_hi = sb("m_hi", [P, HALF, SEQ], F32R)
        m_lo = sb("m_lo", [P, HALF, SEQ], F32R)
        xres = sb("xres", [P, BLOCKS, D_MODEL])
        gate = sb("gate", [P, BLOCKS, 2, WIDTH])
        nat = sb("nat", [P, 2, BLOCKS, WIDTH])
        v_diff = sb("v_diff", [P, BLOCKS, WIDTH])
        v_dsa = sb("v_dsa", [P, BLOCKS, WIDTH])
        ikn = sb("ikn", [P, BLOCKS, IDX_DIM + IDX_HEADS])
        ik2 = sb("ik2", [P, BLOCKS, 2, IDX_DIM])
        iqT = sb("iqT", [P, HEADS, SEQ])
        ikT = sb("ikT", [P, SEQ])
        dqT = sb("dqT", [P, HEADS, SEQ])
        dkT = sb("dkT", [P, HEADS, SEQ])
        sqT = sb("sqT", [P, HEADS, SEQ])
        skT = iqT
        pbuf = sb("pbuf", [P, 4, WIDTH])
        pT = sb("pT", [P, 3, WIDTH])
        mixn = sb("mixn", [P, 2, WIDTH])
        work = [sb("work0", [P, P]), sb("work1", [P, SEQ])]
        top8 = sb("top8", [P, 8])
        chosen = [sb("chosen0", [P, P], BF16), sb("chosen1", [P, SEQ], BF16)]
        prm = sb("prm", [P, ROW_N])
        preT = sb("preT", [P, DEPTH, KT])
        tab = sb("tab", [P, 4, SEQ])
        rt = sb("rt", [P, 2, SEQ])
        trig = sb("trig", [P, 8, BLOCKS * NF])
        frq = sb("frq", [P, NF])
        pos_i = sb("pos_i", [P, BLOCKS], I32)
        pos_f = sb("pos_f", [P, BLOCKS])
        ident = sb("ident", [P, P])
        ident_b = sb("ident_b", [P, P], BF16)
        causal = sb("causal", [P, SEQ])
        causal_b = sb("causal_b", [P, SEQ], BF16)
        st = sb("st", [P, 160])
        neg_half = st[:, 0:8]
        ms_x, rx, ms_y, ry = st[:, 8:10], st[:, 10:12], st[:, 12:14], st[:, 14:16]
        ms_o, ro = st[:, 16:24], st[:, 24:32]
        ep = st[:, 32:48]
        lam_s, lam_e, neg_lam = st[:, 48:50], st[:, 50:52], st[:, 52:53]
        ik_st, ik_mv, ik_r, ik_e = st[:, 56:68], st[:, 68:72], st[:, 72:74], st[:, 74:76]
        iw = st[:, 80:96]
        neg_max = st[:, 96:112]
        sums = st[:, 112:128]
        inv = st[:, 128:144]

        A = [pb("bank_a0", [P, WIDTH]), pb("bank_a1", [P, WIDTH])]
        S = [pb("bank_s0", [P, WIDTH]), pb("bank_s1", [P, WIDTH])]
        T = [pb("bank_t0", [P, WIDTH]), pb("bank_t1", [P, WIDTH])]
        O = [pb("bank_o0", [P, WIDTH]), pb("bank_o1", [P, WIDTH])]

        raw_landed = [count(f"raw_landed{i}", 16 * (UNITS // RING)) for i in range(RING)]
        hi_done = count("hi_done", UNITS)
        lo_done_dve = count("lo_done_dve", UNITS // RING * 3)
        lo_done_pool = count("lo_done_pool", UNITS // RING)
        first_piece = [sem("first_piece_landed"), sem("first_piece_hi")]
        first_half_used = count("first_half_used", CHUNKS)
        out_unit_used = count("out_unit_used", 3, 1)
        proj_done = count("proj_done", GROUPS)
        proj_moved = count("proj_moved", GROUPS)
        y_done = count("y_done", 2, 1)
        y_read = count("y_read", 2, 2)
        x_landed = [sem(f"x_landed{b}") for b in range(BLOCKS)]
        small_landed = sem("small_landed")
        pre_landed = sem("pre_landed")
        prm_landed = count("prm_landed", 16)
        x_ready = count("x_ready", 2 * BLOCKS)
        out_landed = sem("out_landed")
        t_filled = count("t_filled", T_USES)
        t_drained = count("t_drained", T_USES, 1)
        s_filled = count("s_filled", S_USES)
        s_freed = count("s_freed", S_USES)
        s_maxed = count("s_maxed", S_USES - S_DIFF0)
        idx_used = count("idx_used", S_DIFF0)
        o_filled = count("o_filled", 4)
        o_squared = count("o_squared", 2)
        x_squared = count("x_squared", 2)
        y_squared = count("y_squared", 2 * BLOCKS)
        mean_ready = count("mean_ready", 2)
        rx_ready = count("rx_ready", 2)
        ry_ready = count("ry_ready", 2)
        ro_ready = count("ro_ready", 2)
        ik_var = count("ik_var", 1)
        ik_rstd = count("ik_rstd", 1)
        ik_ready = count("ik_ready", 1)
        h_hi_done = count("h_hi_done", 4)
        h_lo_done = count("h_lo_done", 4)
        rope_done = count("rope_done", 5)
        gate_ready = count("gate_ready", 2)
        combined = count("combined", 3)
        mixn_ready = count("mixn_ready", 4, 2)
        chosen_ready = count("chosen_ready", 2)
        lam_summed = count("lam_summed", 1)
        lam_exped = count("lam_exped", 1)
        ident_ready = sem("ident_ready")
        masks_ready = sem("masks_ready")
        angles_ready = sem("angles_ready")
        trig_ready = sem("trig_ready")
        pool_chain = count("pool_chain", POOL_STEPS)
        dve_chain = count("dve_chain", DVE_STEPS)
        pool_setup = sem("pool_setup")

        def chunk_width(u):
            return COLUMNS[u // 2][1] if u < IN_UNITS else WIDTH

        def unit(ring, u):
            return ring[:, u % RING, :, 0:chunk_width(u)]

        def lo_of(u):
            return (lo_done_pool, u // RING + 1) if u % RING == 3 else (lo_done_dve, 3 * (u // RING) + u % RING + 1)

        def weights(layer, u):
            if u < IN_UNITS:
                part, width = COLUMNS[u // 2]
                k0, c0, w = u % 2 * HALF * P, part * WIDTH, w_in
            else:
                width = WIDTH
                k0, c0, w = (u - IN_UNITS) // 2 * HALF * P, (u - IN_UNITS) % 2 * WIDTH, w_out
            return w[layer, k0:k0 + HALF * P, c0:c0 + width].rearrange("(k p) n -> p k n", p=P)

        def param(name):
            a, b = AT[name]
            return prm[:, a:b]

        subln = param("subln")
        y_w = pbuf[:, :, :].rearrange("p (b a) n -> p b (a n)", b=BLOCKS)
        ik_tmp = pbuf[:, 1, 0:2 * BLOCKS * 2 * HD].rearrange("p (t b d) -> p t b d", t=2, b=BLOCKS)
        block = ctx.enter_context(nc.Block())

        @block.sync
        def _(sp):
            sp.dma_start(xres[:, 0, :], x[0, 0:P, :]).then_inc(x_landed[0], 16)
            sp.dma_start(raw[:, 0, 0:2, :], weights(0, 0)[:, 0:2, :]).then_inc(first_piece[0], 16)
            sp.dma_start(raw[:, 0, 2:HALF, :], weights(0, 0)[:, 2:HALF, :]).then_inc(raw_landed[0].sem, 16)
            sp.dma_start(xres[:, 1, :], x[0, P:SEQ, :]).then_inc(x_landed[1], 16)
            for u in range(1, RING):
                sp.dma_start(unit(raw, u), weights(0, u)).then_inc(raw_landed[u].sem, 16)
            sp.dma_start(prm[:, :], rows[0:1, :].to_broadcast([P, ROW_N])).then_inc(prm_landed.sem, 16)
            for layer in range(DEPTH):
                for u in range(UNITS - RING):
                    done, n = lo_of(u)
                    sp.wait_ge(done.sem, done.at(layer, n))
                    sp.dma_start(unit(raw, u + RING), weights(layer, u + RING)).then_inc(raw_landed[u % RING].sem, 16)
                if layer < DEPTH - 1:
                    for u in range(RING):
                        done, n = lo_of(UNITS - RING + u)
                        sp.wait_ge(done.sem, done.at(layer, n))
                        sp.dma_start(unit(raw, u), weights(layer + 1, u)).then_inc(raw_landed[u].sem, 16)
                    sp.wait_ge(y_read.sem, y_read.at(layer, 2))
                    sp.dma_start(prm[:, :], rows[layer + 1:layer + 2, :].to_broadcast([P, ROW_N])).then_inc(prm_landed.sem, 16)
            for b in range(BLOCKS):
                for n in range(2):
                    part = slice(n * WIDTH, (n + 1) * WIDTH)
                    sp.wait_ge(x_ready.sem, x_ready.at(DEPTH, 2 * b + n + 1))
                    sp.dma_start(out[0, b * P:(b + 1) * P, part], xres[:, b, part]).then_inc(out_landed, 16)
            sp.wait_ge(out_landed, 16 * 2 * BLOCKS)

        @block.tensor
        def _(pe):
            def turn_x(layer, b):
                for n in range(2):
                    pe.wait_ge(x_ready.sem, x_ready.at(layer, 2 * b + n + 1))
                    pe.wait_ge(t_drained.sem, t_drained.at(layer, max(2 * b + n - 1, 0)))
                    for k in range(HALF):
                        at = (HALF * n + k) * P
                        mm = pe.transpose(T[n][:, k * P:(k + 1) * P], xres[:, b, at:at + P], ident[:, :])
                    mm.then_inc(t_filled.sem, 1)

            def body(layer):
                def bank_t(j):
                    pe.wait_ge(t_drained.sem, t_drained.at(layer, j - 1))
                    return T[j % 2]

                def bank_s(j):
                    if j < 2:
                        pe.wait_ge(y_read.sem, y_read.at(layer, 0))
                    else:
                        pe.wait_ge(s_freed.sem, s_freed.at(layer, j - 1))
                    return S[j % 2]

                def turn(j, parts):
                    bank = bank_t(j)
                    for n, part in enumerate(parts):
                        mm = pe.transpose(bank[:, n * P:(n + 1) * P], part, ident[:, :])
                    mm.then_inc(t_filled.sem, 1)

                def turn_nat(j, slot, rope):
                    pe.wait_ge(rope_done.sem, rope_done.at(layer, rope))
                    for n in range(2):
                        turn(j + n, [nat[:, slot, b, f * P:(f + 1) * P] for f in (2 * n, 2 * n + 1) for b in range(BLOCKS)])

                def part_of(g, half):
                    chunk, b = order(layer)[g]
                    u, width, tok = 2 * chunk + half, COLUMNS[chunk][1], slice(b * P, (b + 1) * P)
                    bank = A[g % 2][:, 0:width]
                    whi, wlo = unit(w_hi, u), unit(w_lo, u)
                    pe.wait_ge(hi_done.sem, hi_done.at(layer, u + 1))
                    pe.wait_ge(h_hi_done.sem, h_hi_done.at(layer, 2 * b + half + 1))
                    for kk in range(HALF):
                        pe.matmul(bank, h_hi[:, HALF * half + kk, tok], whi[:, kk, :], start=half == 0 and kk == 0, stop=False)
                    pe.wait_ge(h_lo_done.sem, h_lo_done.at(layer, 2 * b + half + 1))
                    for kk in range(HALF):
                        pe.matmul(bank, h_lo[:, HALF * half + kk, tok], whi[:, kk, :], start=False, stop=False)
                    done, n = lo_of(u)
                    pe.wait_ge(done.sem, done.at(layer, n))
                    for kk in range(HALF):
                        mm = pe.matmul(bank, h_hi[:, HALF * half + kk, tok], wlo[:, kk, :], start=False,
                                       stop=half == 1 and kk == HALF - 1)
                    return mm

                def first(g):
                    if g < 2:
                        pe.wait_ge(y_read.sem, y_read.at(layer, -1))
                    else:
                        pe.wait_ge(proj_moved.sem, proj_moved.at(layer, g - 1))
                    mm = part_of(g, 0)
                    if order(layer)[g][1] == 1:
                        mm.then_inc(first_half_used.sem, 1)

                def second(g):
                    part_of(g, 1).then_inc(proj_done.sem, 1)

                def index_logits(j, b, heads):
                    bank, n = bank_s(j), P * (b + 1)
                    for i, h in enumerate(heads):
                        rows_h = slice(IDX_DIM * (h % 2), IDX_DIM * (h % 2 + 1))
                        mm = pe.matmul(bank[:, i * n:(i + 1) * n], iqT[rows_h, h // 2, b * P:(b + 1) * P],
                                       ikT[rows_h, 0:n], start=True, stop=True)
                    mm.then_inc(s_filled.sem, 1)

                def mask_bank(bank, masks, b):
                    n = P * (b + 1)
                    for i, m in enumerate(masks):
                        pe.matmul(bank[:, :].rearrange("p (r k) -> p r k", k=n), ident_b[:, :],
                                  m[:, None, :].to_broadcast([P, WIDTH // n, n]), start=(i == 0), stop=False)

                def diff_scores(j, b, heads):
                    bank, n, m = bank_s(j), P * (b + 1), j % 2
                    mask_bank(bank, [causal_b[:, P:SEQ] if b == 0 else causal_b[:, :]], b)
                    for i, h in enumerate(heads):
                        rows_m = slice(DIFF_QK * m, DIFF_QK * (m + 1))
                        mm = pe.matmul(bank[:, i * n:(i + 1) * n], dqT[rows_m, h, b * P:(b + 1) * P],
                                       dkT[rows_m, h, 0:n], start=False, stop=(i == len(heads) - 1))
                    mm.then_inc(s_filled.sem, 1)

                def dsa_scores(j, b, heads):
                    bank, n = bank_s(j), P * (b + 1)
                    pe.wait_ge(chosen_ready.sem, chosen_ready.at(layer, b + 1))
                    mask_bank(bank, [chosen[b][:, :]] + ([causal_b[:, P:SEQ]] if b == 0 else []), b)
                    for i, h in enumerate(heads):
                        mm = pe.matmul(bank[:, i * n:(i + 1) * n], sqT[:, h, b * P:(b + 1) * P],
                                       skT[:, h, 0:n], start=False, stop=(i == len(heads) - 1))
                    mm.then_inc(s_filled.sem, 1)

                def turn_probs(j, use, b, heads):
                    n = P * (b + 1)
                    turn(j, [pbuf[:, use % 4, i * n + t * P:i * n + (t + 1) * P] for i in range(heads) for t in range(b + 1)])

                def values(o, b, v, tiles, drained, moved):
                    pe.wait_ge(t_drained.sem, t_drained.at(layer, drained))
                    pe.wait_ge(proj_moved.sem, proj_moved.at(layer, moved))
                    pe.wait_ge(mixn_ready.sem, mixn_ready.at(layer, o - 1))
                    for h, parts in enumerate(tiles):
                        for t, part in enumerate(parts):
                            mm = pe.matmul(O[o % 2][:, h * E:(h + 1) * E], part, v[:, t, h * E:(h + 1) * E],
                                           start=(t == 0), stop=(t == len(parts) - 1))
                    mm.then_inc(o_filled.sem, 1)

                def slot(i, n):
                    return pT[:, i, n * P:(n + 1) * P]

                def turn_mix(j, i, o):
                    pe.wait_ge(mixn_ready.sem, mixn_ready.at(layer, o + 1))
                    turn(j, [mixn[:, i, k * P:(k + 1) * P] for k in range(HALF)])

                def out_part(half, b, n):
                    x_hi, x_lo = (m_hi, m_lo) if half == 0 else (h_hi, h_lo)
                    u, tok = IN_UNITS + 2 * half + n, slice(b * P, (b + 1) * P)
                    bank = (A, S)[b][n][:, :]
                    done, at = lo_of(u)
                    pe.wait_ge(done.sem, done.at(layer, at))
                    for i, (x, w) in enumerate(((x_hi, w_hi), (x_lo, w_hi), (x_hi, w_lo))):
                        for kk in range(HALF):
                            mm = pe.matmul(bank, x[:, kk, tok], w[:, u % RING, kk, :], start=half == 0 and i == 0 and kk == 0,
                                           stop=half == 1 and i == 2 and kk == HALF - 1)
                    return mm

                if layer == 0:
                    turn_x(layer, 1)
                    first(0)
                    first(1)
                    second(0)
                    pe.wait_ge(masks_ready, 1)
                    second(1)
                else:
                    first(0)
                    second(0)
                    turn_x(layer, 1)
                    first(1)
                    second(1)
                for g in range(2, 9):
                    first(g)
                    second(g)
                turn_nat(T_IQ, 0, 1)
                first(9)
                pe.wait_ge(ik_ready.sem, ik_ready.at(layer, 1))
                turn(T_IK, [ik2[:, b, :, :].rearrange("p t d -> p (t d)") for b in range(BLOCKS)])
                second(9)
                first(10)
                pe.wait_ge(t_drained.sem, t_drained.at(layer, T_IK + 1))
                index_logits(0, 0, (0, 2, 4, 6))
                index_logits(1, 0, (1, 3, 5, 7))
                second(10)
                index_logits(2, 1, (0, 2))
                index_logits(3, 1, (1, 3))
                first(11)
                turn_nat(T_DQ, 1, 2)
                index_logits(4, 1, (4, 6))
                index_logits(5, 1, (5, 7))
                second(11)
                first(12)
                second(12)
                turn_nat(T_DK, 0, 3)
                first(13)
                pe.wait_ge(t_drained.sem, t_drained.at(layer, T_DK + 2))
                diff_scores(6, 0, range(HEADS))
                diff_scores(7, 0, range(HEADS))
                second(13)
                first(14)
                diff_scores(8, 1, (0, 1))
                diff_scores(9, 1, (0, 1))
                second(14)
                turn_nat(T_SQ, 1, 4)
                first(15)
                pe.wait_ge(combined.sem, combined.at(layer, 1))
                turn_probs(T_PD0, 6, 0, HEADS)
                diff_scores(10, 1, (2, 3))
                diff_scores(11, 1, (2, 3))
                second(15)
                pe.wait_ge(combined.sem, combined.at(layer, 2))
                turn_probs(T_PD1A, 8, 1, 2)
                first(16)
                second(16)
                turn_nat(T_SK, 0, 5)
                first(17)
                pe.wait_ge(combined.sem, combined.at(layer, 3))
                turn_probs(T_PD1B, 10, 1, 2)
                pe.wait_ge(t_drained.sem, t_drained.at(layer, T_SK + 2))
                dsa_scores(12, 0, range(HEADS))
                values(0, 0, v_diff, [[slot(0, h)] for h in range(HEADS)], T_PD0 + 1, place(layer, DV, 0) + 1)
                second(17)
                first(18)
                dsa_scores(13, 1, (0, 1))
                dsa_scores(14, 1, (2, 3))
                values(1, 1, v_diff, [[slot(1 + h // 2, 2 * (h % 2) + t) for t in range(2)] for h in range(HEADS)],
                       T_PD1B + 1, place(layer, DV, 1) + 1)
                second(18)
                turn_mix(T_MD0, 0, 0)
                first(19)
                pe.wait_ge(s_freed.sem, s_freed.at(layer, 13))
                turn_probs(T_PS0, 12, 0, HEADS)
                second(19)
                turn_mix(T_MD1, 1, 1)
                values(2, 0, v_dsa, [[slot(0, h)] for h in range(HEADS)], T_PS0 + 1, place(layer, SV, 0) + 1)
                pe.wait_ge(s_freed.sem, s_freed.at(layer, 15))
                turn_probs(T_PS1A, 13, 1, 2)
                pe.wait_ge(t_drained.sem, t_drained.at(layer, T_MD0 + 1))
                out_part(0, 0, 0)
                turn_probs(T_PS1B, 14, 1, 2)
                turn_mix(T_MS0, 0, 2)
                pe.wait_ge(proj_moved.sem, proj_moved.at(layer, GROUPS))
                out_part(0, 0, 1)
                values(3, 1, v_dsa, [[slot(1 + h // 2, 2 * (h % 2) + t) for t in range(2)] for h in range(HEADS)],
                       T_PS1B + 1, place(layer, SV, 1) + 1)
                pe.wait_ge(t_drained.sem, t_drained.at(layer, T_MS0 + 1))
                out_part(1, 0, 0)
                out_part(1, 0, 1).then_inc(y_done.sem, 1)
                pe.wait_ge(t_drained.sem, t_drained.at(layer, T_MD1 + 1))
                out_part(0, 1, 0).then_inc(out_unit_used.sem, 1)
                turn_mix(T_MS1, 1, 3)
                out_part(0, 1, 1).then_inc(out_unit_used.sem, 1)
                pe.wait_ge(t_drained.sem, t_drained.at(layer, T_MS1 + 1))
                out_part(1, 1, 0).then_inc(out_unit_used.sem, 1)
                if layer < DEPTH - 1:
                    turn_x(layer + 1, 0)
                out_part(1, 1, 1).then_inc(y_done.sem, 1)

            pe.wait_ge(ident_ready, 1)
            turn_x(0, 0)
            for layer in range(DEPTH):
                body(layer)

        @block.scalar
        def _(act):
            def split_hi(layer, u):
                if u >= RING:
                    v = u - RING
                    if v % 2 == 0:
                        act.wait_ge(first_half_used.sem, first_half_used.at(layer, v // 2 + 1))
                    else:
                        act.wait_ge(proj_done.sem, proj_done.at(layer, place(layer, v // 2, 1) + 1))
                act.wait_ge(raw_landed[u % RING].sem, raw_landed[u % RING].at(layer, 16 * (u // RING + 1)))
                act.activation(unit(w_hi, u), unit(raw, u), ACT.Copy).then_inc(hi_done.sem, 1)

            def x_hi(layer, b):
                for n in range(2):
                    j = 2 * b + n
                    act.wait_ge(t_drained.sem, t_drained.at(layer, j + 1))
                    act.activation(h_hi[:, HALF * n:HALF * (n + 1), b * P:(b + 1) * P],
                                   pT[:, j % 3, :].rearrange("p (k t) -> p k t", k=HALF), ACT.Copy).then_inc(h_hi_done.sem, 1)

            def square_x(layer, b):
                act.wait_ge(x_ready.sem, x_ready.at(layer, 2 * b + 2))
                act.activation(nat[:, b, :, :].rearrange("p a n -> p (a n)"), xres[:, b, :], ACT.Square,
                               accum_out=ms_x[:, b:b + 1]).then_inc(x_squared.sem, 1)

            def body(layer):
                def move(g):
                    chunk, b = order(layer)[g]
                    width = COLUMNS[chunk][1]
                    dst = {DG: gate[:, b, 0, :], SG: gate[:, b, 1, :], TAIL: ikn[:, b, :], DV: v_diff[:, b, :],
                           SV: v_dsa[:, b, :], IQ: nat[:, 0, b, :], DQ: nat[:, 1, b, :], DK: nat[:, 0, b, :],
                           SQ: nat[:, 1, b, :], SK: nat[:, 0, b, :]}[chunk]
                    act.wait_ge(proj_done.sem, proj_done.at(layer, g + 1))
                    if g == place(layer, 0, b):
                        act.wait_ge(rx_ready.sem, rx_ready.at(layer, b + 1))
                    act.activation(dst, A[g % 2][:, 0:width], ACT.Silu if chunk in (DG, SG) else ACT.Copy,
                                   scale=rx[:, b:b + 1]).then_inc(proj_moved.sem, 1)

                def relu(j):
                    act.wait_ge(s_filled.sem, s_filled.at(layer, j + 1))
                    if j >= 4:
                        act.wait_ge(idx_used.sem, idx_used.at(layer, j - 3))
                    act.activation(pbuf[:, j % 4, :], S[j % 2][:, :], ACT.Relu).then_inc(s_freed.sem, 1)

                def exps(j, b, n_rows):
                    n, r = P * (b + 1), 4 * (j % 4)
                    act.wait_ge(s_maxed.sem, s_maxed.at(layer, j - S_DIFF0 + 1))
                    if j in (10, 11):
                        act.wait_ge(t_filled.sem, t_filled.at(layer, T_PD0 + 1))
                    for i in range(n_rows):
                        ins = act.activation(pbuf[:, j % 4, i * n:(i + 1) * n], S[j % 2][:, i * n:(i + 1) * n], ACT.Exp,
                                             bias=neg_max[:, r + i:r + i + 1], accum_out=sums[:, r + i:r + i + 1])
                    ins.then_inc(s_freed.sem, 1)

                def square_o(b):
                    act.wait_ge(o_filled.sem, o_filled.at(layer, b + 1))
                    for h in range(HEADS):
                        ins = act.activation(mixn[:, b, h * E:(h + 1) * E], O[b][:, h * E:(h + 1) * E], ACT.Square,
                                             accum_out=ms_o[:, HEADS * b + h:HEADS * b + h + 1])
                    ins.then_inc(o_squared.sem, 1)

                def square_y(b):
                    bank = (A, S)[b]
                    for n in range(2):
                        if (b, n) == (1, 0):
                            act.wait_ge(out_unit_used.sem, out_unit_used.at(layer, 3))
                        else:
                            act.wait_ge(y_done.sem, y_done.at(layer, b + 1))
                        act.activation(nat[:, b, n, :], bank[n][:, :], ACT.Square,
                                       accum_out=ep[:, 2 * b + n:2 * b + n + 1]).then_inc(y_squared.sem, 1)

                act.wait_ge(y_done.sem, y_done.at(layer, 0))
                split_hi(layer, 3)
                if layer:
                    square_x(layer, 1)
                move(0)
                if layer:
                    x_hi(layer, 1)
                move(1)
                split_hi(layer, 4)
                if layer == 0:
                    split_hi(layer, 5)
                move(2)
                if layer:
                    split_hi(layer, 5)
                split_hi(layer, 6)
                move(3)
                split_hi(layer, 7)
                for g in range(5, 10):
                    move(g - 1)
                    split_hi(layer, g + 3)
                move(9)
                split_hi(layer, 13)
                relu(0)
                relu(1)
                move(10)
                relu(2)
                relu(3)
                split_hi(layer, 14)
                relu(4)
                relu(5)
                move(11)
                act.wait_ge(lam_summed.sem, lam_summed.at(layer, 1))
                act.activation(lam_e, lam_s, ACT.Exp).then_inc(lam_exped.sem, 1)
                split_hi(layer, 15)
                move(12)
                split_hi(layer, 16)
                exps(6, 0, 4)
                exps(7, 0, 4)
                move(13)
                split_hi(layer, 17)
                exps(8, 1, 2)
                exps(9, 1, 2)
                move(14)
                split_hi(layer, 18)
                exps(10, 1, 2)
                exps(11, 1, 2)
                move(15)
                split_hi(layer, 19)
                move(16)
                split_hi(layer, 20)
                exps(12, 0, 4)
                move(17)
                square_o(0)
                split_hi(layer, 21)
                exps(13, 1, 2)
                exps(14, 1, 2)
                square_o(1)
                move(18)
                split_hi(layer, 22)
                move(19)
                split_hi(layer, 23)
                square_y(0)
                if layer < DEPTH - 1:
                    act.wait_ge(out_unit_used.sem, out_unit_used.at(layer, 1))
                    split_hi(layer + 1, 0)
                    act.wait_ge(out_unit_used.sem, out_unit_used.at(layer, 2))
                    split_hi(layer + 1, 1)
                    act.wait_ge(out_unit_used.sem, out_unit_used.at(layer, 3))
                    split_hi(layer + 1, 2)
                    x_hi(layer + 1, 0)
                    square_x(layer + 1, 0)
                square_y(1)

            act.dma_start(preT[:, :, :], pre_t.rearrange("p (l k) -> p l k", l=DEPTH)).then_inc(pre_landed, 16)
            act.dma_start(pos_i[:, :], positions).then_inc(small_landed, 16)
            act.dma_start(frq[:, :], freqs.to_broadcast([P, NF])).then_inc(small_landed, 16)
            act.wait_ge(first_piece[0], 16)
            act.activation(w_hi[:, 0, 0:2, :], raw[:, 0, 0:2, :], ACT.Copy).then_inc(first_piece[1], 1)
            x_hi(0, 0)
            act.wait_ge(raw_landed[0].sem, 16)
            act.activation(w_hi[:, 0, 2:HALF, :], raw[:, 0, 2:HALF, :], ACT.Copy).then_inc(hi_done.sem, 1)
            square_x(0, 0)
            x_hi(0, 1)
            split_hi(0, 1)
            square_x(0, 1)
            act.wait_ge(angles_ready, 1)
            act.activation(trig[:, 4:6, :], trig[:, 2:4, :], ACT.Sin).then_inc(trig_ready, 1)
            split_hi(0, 2)
            for layer in range(DEPTH):
                body(layer)

        @block.vector
        def _(dve):
            steps = [0]

            def split_lo(layer, u):
                dve.wait_ge(hi_done.sem, hi_done.at(layer, u + 1))
                dve.tensor_tensor(unit(w_lo, u), unit(raw, u), unit(w_hi, u).bitcast(F32), ALU.subtract).then_inc(lo_done_dve.sem, 1)

            def drain_x(layer, b):
                for n in range(2):
                    j = 2 * b + n
                    dve.wait_ge(t_filled.sem, t_filled.at(layer, j + 1))
                    if j == 3:
                        dve.wait_ge(h_lo_done.sem, h_lo_done.at(layer, 1))
                    w = preT[:, layer, HALF * n:HALF * (n + 1)][:, :, None].to_broadcast([P, HALF, P])
                    dve.tensor_tensor(pT[:, j % 3, :].rearrange("p (k t) -> p k t", k=HALF),
                                      T[j % 2][:, :].rearrange("p (k t) -> p k t", k=HALF), w, ALU.mult).then_inc(t_drained.sem, 1)
                for n in range(2):
                    j = 2 * b + n
                    dve.wait_ge(h_hi_done.sem, h_hi_done.at(layer, j + 1))
                    part = (slice(None), slice(HALF * n, HALF * (n + 1)), slice(b * P, (b + 1) * P))
                    dve.tensor_tensor(h_lo[part], pT[:, j % 3, :].rearrange("p (k t) -> p k t", k=HALF),
                                      h_hi[part].bitcast(F32), ALU.subtract).then_inc(h_lo_done.sem, 1)

            def body(layer):
                steps[0] = 0

                def mark(ins):
                    steps[0] += 1
                    ins.then_inc(dve_chain.sem, 1)

                def settle():
                    dve.wait_ge(dve_chain.sem, dve_chain.at(layer, steps[0]))

                def link(ins):
                    mark(ins)
                    settle()

                def drain(j, dst, scale=None):
                    dve.wait_ge(t_filled.sem, t_filled.at(layer, j + 1))
                    if scale is None:
                        ins = dve.tensor_copy(dst, T[j % 2][:, 0:dst.free_size()])
                    else:
                        ins = dve.tensor_scalar(dst, T[j % 2][:, :], scale, None, ALU.mult)
                    ins.then_inc(t_drained.sem, 1)

                def drain_pair(j, dst, scale=None):
                    for n in range(2):
                        drain(j + n, dst[:, 2 * n:2 * n + 2, :].rearrange("p f t -> p (f t)"), scale)

                def drain_mix(j, dst_hi, dst_lo, b):
                    dve.wait_ge(t_filled.sem, t_filled.at(layer, j + 1))
                    part = (slice(None), slice(0, HALF), slice(b * P, (b + 1) * P))
                    src = T[j % 2][:, :].rearrange("p (k t) -> p k t", k=HALF)
                    link(dve.tensor_copy(dst_hi[part], src))
                    dve.tensor_tensor(dst_lo[part], src, dst_hi[part].bitcast(F32), ALU.subtract).then_inc(t_drained.sem, 1)

                def index_key():
                    dve.wait_ge(proj_moved.sem, proj_moved.at(layer, place(layer, TAIL, 1) + 1))
                    for b in range(BLOCKS):
                        mark(dve.bn_stats(ik_st[:, 6 * b:6 * b + 6], ikn[:, b, 0:IDX_DIM]))
                    mark(dve.tensor_scalar(iw.rearrange("p (b h) -> p b h", b=BLOCKS), ikn[:, :, IDX_DIM:IDX_DIM + IDX_HEADS],
                                           IDX_HEADS ** -0.5 * IDX_DIM ** -0.5, None, ALU.mult))
                    settle()
                    for b in range(BLOCKS):
                        ins = dve.bn_aggr(ik_mv[:, 2 * b:2 * b + 2], ik_st[:, 6 * b:6 * b + 6])
                        if b == 0:
                            mark(ins)
                    ins.then_inc(ik_var.sem, 1)
                    dve.wait_ge(ik_rstd.sem, ik_rstd.at(layer, 1))
                    k = ik2[:, :, 0, :]
                    for b in range(BLOCKS):
                        mark(dve.tensor_scalar(ik2[:, b, 0, :], ikn[:, b, 0:IDX_DIM], ik_mv[:, 2 * b:2 * b + 1],
                                               ik_r[:, b:b + 1], ALU.subtract, ALU.mult))
                    settle()
                    wide = [P, BLOCKS, IDX_DIM]
                    link(dve.tensor_tensor(k, k, param("ik_w")[:, None, :].to_broadcast(wide), ALU.mult))
                    link(dve.tensor_tensor(k, k, param("ik_b")[:, None, :].to_broadcast(wide), ALU.add))
                    cos = tab[:, 0, :].rearrange("p (b h d) -> p b h d", b=BLOCKS, d=2 * HD)[:, :, 0, :]
                    sin = tab[:, 1, :].rearrange("p (b h d) -> p b h d", b=BLOCKS, d=2 * HD)[:, :, 0, :]
                    c = ik_tmp[:, 0]
                    s = ik_tmp[:, 1]
                    mark(dve.tensor_tensor(c, k[:, :, 0:2 * HD], cos, ALU.mult))
                    mark(dve.tensor_tensor(s[:, :, 0:HD], k[:, :, HD:2 * HD], sin[:, :, 0:HD], ALU.mult))
                    mark(dve.tensor_tensor(s[:, :, HD:2 * HD], k[:, :, 0:HD], sin[:, :, HD:2 * HD], ALU.mult))
                    settle()
                    link(dve.tensor_tensor(k[:, :, 0:2 * HD], c, s, ALU.add))
                    dve.tensor_copy(ik2[:, :, 1, :], k).then_inc(ik_ready.sem, 1)

                def index_sum(j, b, heads):
                    dve.wait_ge(s_freed.sem, s_freed.at(layer, j + 1))
                    n = P * (b + 1)
                    for i, h in enumerate(heads):
                        first = causal[:, P:SEQ] if b == 0 else causal[:, :]
                        ins = dve.scalar_tensor_tensor(out=work[b][:, :], in0=pbuf[:, j % 4, i * n:(i + 1) * n],
                                                       scalar=iw[:, IDX_HEADS * b + h:IDX_HEADS * b + h + 1],
                                                       in1=first if h == 0 else work[b][:, :], op0=ALU.mult, op1=ALU.add)
                        if i < len(heads) - 1:
                            link(ins)
                    ins.then_inc(idx_used.sem, 1)
                    dve.wait_ge(idx_used.sem, idx_used.at(layer, j + 1))

                def choose(b, rounds):
                    for _ in range(rounds):
                        link(dve.max(top8[:, :], work[b][:, :]))
                        link(dve.match_replace(work[b][:, :], top8[:, :], work[b][:, :], TAKEN))

                def chosen_mask(b):
                    dve.tensor_scalar(chosen[b][:, :], work[b][:, :], TAKEN_ABOVE, NEG, ALU.is_gt, ALU.mult).then_inc(chosen_ready.sem, 1)

                def row_max(j, b, n_rows):
                    dve.wait_ge(s_filled.sem, s_filled.at(layer, j + 1))
                    r = 4 * (j % 4)
                    dve.tensor_reduce(neg_max[:, r:r + n_rows], S[j % 2][:, :].rearrange("p (r k) -> p r k", r=n_rows),
                                      AX.X, ALU.max, negate=True).then_inc(s_maxed.sem, 1)

                def combine(j, b, n_heads):
                    n, r = P * (b + 1), 4 * (j % 4)
                    dve.wait_ge(s_freed.sem, s_freed.at(layer, j + 2))
                    for at in (r, r + 4):
                        mark(dve.reciprocal(inv[:, at:at + n_heads], sums[:, at:at + n_heads]))
                    settle()
                    link(dve.tensor_scalar(inv[:, r + 4:r + 4 + n_heads], inv[:, r + 4:r + 4 + n_heads], neg_lam, None, ALU.mult))
                    for i in range(n_heads):
                        p1 = pbuf[:, j % 4 + 1, i * n:(i + 1) * n]
                        mark(dve.tensor_scalar(p1, p1, inv[:, r + 4 + i:r + 5 + i], None, ALU.mult))
                    settle()
                    for i in range(n_heads):
                        p0 = pbuf[:, j % 4, i * n:(i + 1) * n]
                        p1 = pbuf[:, j % 4 + 1, i * n:(i + 1) * n]
                        ins = dve.scalar_tensor_tensor(out=p0, in0=p0, scalar=inv[:, r + i:r + i + 1], in1=p1, op0=ALU.mult, op1=ALU.add)
                        if i < n_heads - 1:
                            mark(ins)
                    ins.then_inc(combined.sem, 1)

                def gated(o, scalars):
                    b, mixer = o % 2, o // 2
                    for h in range(HEADS):
                        part = slice(h * E, (h + 1) * E)
                        ins = dve.scalar_tensor_tensor(out=mixn[:, b, part], in0=O[b][:, part], scalar=scalars[h],
                                                       in1=gate[:, b, mixer, part], op0=ALU.mult, op1=ALU.mult)
                    ins.then_inc(mixn_ready.sem, 1)

                def gate_diff(b):
                    dve.wait_ge(ro_ready.sem, ro_ready.at(layer, b + 1))
                    if b == 0:
                        dve.wait_ge(gate_ready.sem, gate_ready.at(layer, 2))
                    gated(b, [ro[:, HEADS * b + h:HEADS * b + h + 1] for h in range(HEADS)])

                def gate_dsa(b):
                    for use in ((12,), (13, 14))[b]:
                        r, n = 4 * (use % 4), 4 if b == 0 else 2
                        mark(dve.reciprocal(inv[:, r:r + n], sums[:, r:r + n]))
                    settle()
                    dve.wait_ge(o_filled.sem, o_filled.at(layer, 3 + b))
                    gated(2 + b, [inv[:, (h if b == 0 else 4 * (1 + h // 2) + h % 2):][:, 0:1] for h in range(HEADS)])

                def weight_y(b):
                    for n in range(2):
                        dve.wait_ge(y_squared.sem, y_squared.at(layer, 2 * b + n + 1))
                        part = slice(n * WIDTH, (n + 1) * WIDTH)
                        ins = dve.tensor_tensor(y_w[:, b, part], (A, S)[b][n][:, :], param("post")[:, part], ALU.mult)
                    ins.then_inc(y_read.sem, 1)

                def residual(b):
                    dve.wait_ge(y_read.sem, y_read.at(layer, b + 1))
                    dve.wait_ge(ry_ready.sem, ry_ready.at(layer, b + 1))
                    for n in range(2):
                        part = slice(n * WIDTH, (n + 1) * WIDTH)
                        dve.scalar_tensor_tensor(out=xres[:, b, part], in0=y_w[:, b, part], scalar=ry[:, b:b + 1],
                                                 in1=xres[:, b, part], op0=ALU.mult, op1=ALU.add).then_inc(x_ready.sem, 1)

                if layer:
                    drain_x(layer, 1)
                split_lo(layer, 4)
                dve.wait_ge(prm_landed.sem, prm_landed.at(layer, 16))
                lam_a, lam_b = pbuf[:, 0, 0:DIFF_QK], pbuf[:, 0, DIFF_QK:2 * DIFF_QK]
                mark(dve.tensor_tensor_reduce(lam_a, param("lq1"), param("lk1"), 1.0, 0.0, ALU.mult, ALU.add, lam_s[:, 0:1]))
                dve.tensor_tensor_reduce(lam_b, param("lq2"), param("lk2"), 1.0, 0.0, ALU.mult, ALU.add, lam_s[:, 1:2]).then_inc(lam_summed.sem, 1)
                split_lo(layer, 5)
                split_lo(layer, 6)
                split_lo(layer, 8)
                split_lo(layer, 9)
                split_lo(layer, 10)
                index_key()
                drain_pair(T_IQ, iqT)
                split_lo(layer, 12)
                drain(T_IK, ikT[:, :])
                split_lo(layer, 13)
                index_sum(0, 0, (0, 2, 4, 6))
                index_sum(1, 0, (1, 3, 5, 7))
                index_sum(2, 1, (0, 2))
                index_sum(3, 1, (1, 3))
                drain_pair(T_DQ, dqT, DIFF_QK ** -0.5)
                split_lo(layer, 14)
                index_sum(4, 1, (4, 6))
                index_sum(5, 1, (5, 7))
                choose(0, 8)
                chosen_mask(0)
                drain_pair(T_DK, dkT)
                choose(1, 3)
                row_max(6, 0, 4)
                row_max(7, 0, 4)
                split_lo(layer, 16)
                dve.wait_ge(lam_exped.sem, lam_exped.at(layer, 1))
                link(dve.tensor_tensor(neg_lam, lam_e[:, 1:2], lam_e[:, 0:1], ALU.subtract))
                link(dve.tensor_tensor(neg_lam, neg_lam, param("lam_init"), ALU.subtract))
                combine(6, 0, HEADS)
                row_max(8, 1, 2)
                row_max(9, 1, 2)
                split_lo(layer, 17)
                drain_pair(T_SQ, sqT, E ** -0.5)
                combine(8, 1, 2)
                drain(T_PD0, pT[:, 0, :])
                row_max(10, 1, 2)
                row_max(11, 1, 2)
                choose(1, 2)
                combine(10, 1, 2)
                drain(T_PD1A, pT[:, 1, :])
                choose(1, 3)
                chosen_mask(1)
                drain_pair(T_SK, skT)
                split_lo(layer, 18)
                drain(T_PD1B, pT[:, 2, :])
                row_max(12, 0, 4)
                split_lo(layer, 20)
                gate_diff(0)
                split_lo(layer, 21)
                row_max(13, 1, 2)
                row_max(14, 1, 2)
                drain_mix(T_MD0, m_hi, m_lo, 0)
                gate_diff(1)
                drain(T_PS0, pT[:, 0, :])
                split_lo(layer, 22)
                drain_mix(T_MD1, m_hi, m_lo, 1)
                drain(T_PS1A, pT[:, 1, :])
                gate_dsa(0)
                drain(T_PS1B, pT[:, 2, :])
                drain_mix(T_MS0, h_hi, h_lo, 0)
                gate_dsa(1)
                weight_y(0)
                residual(0)
                drain_mix(T_MS1, h_hi, h_lo, 1)
                if layer < DEPTH - 1:
                    split_lo(layer + 1, 0)
                    drain_x(layer + 1, 0)
                    split_lo(layer + 1, 1)
                    split_lo(layer + 1, 2)
                weight_y(1)
                residual(1)
                assert steps[0] == DVE_STEPS, steps[0]

            dve.nop().then_inc(out_unit_used.sem, out_unit_used.before)
            dve.nop().then_inc(y_done.sem, y_done.before)
            dve.nop().then_inc(y_read.sem, y_read.before)
            dve.nop().then_inc(t_drained.sem, t_drained.before)
            dve.nop().then_inc(mixn_ready.sem, mixn_ready.before)
            dve.wait_ge(x_landed[0], 16)
            dve.nop().then_inc(x_ready.sem, 2)
            dve.wait_ge(pre_landed, 16)
            drain_x(0, 0)
            dve.wait_ge(first_piece[1], 1)
            dve.tensor_tensor(w_lo[:, 0, 0:2, :], raw[:, 0, 0:2, :], w_hi[:, 0, 0:2, :].bitcast(F32), ALU.subtract)
            dve.wait_ge(hi_done.sem, 1)
            dve.tensor_tensor(w_lo[:, 0, 2:HALF, :], raw[:, 0, 2:HALF, :], w_hi[:, 0, 2:HALF, :].bitcast(F32), ALU.subtract).then_inc(lo_done_dve.sem, 1)
            dve.wait_ge(x_landed[1], 16)
            dve.nop().then_inc(x_ready.sem, 2)
            drain_x(0, 1)
            split_lo(0, 1)
            split_lo(0, 2)
            for layer in range(DEPTH):
                body(layer)

        @block.gpsimd
        def _(pool):
            steps, setup = [0], [0]

            def root_x(layer, b):
                pool.wait_ge(x_squared.sem, x_squared.at(layer, b + 1))
                mean = ep[:, 4 + b:5 + b]
                pool.tensor_scalar(mean, ms_x[:, b:b + 1], 1.0 / D_MODEL, NORM_EPS, ALU.mult, ALU.add).then_inc(mean_ready.sem, 1)
                pool.wait_ge(mean_ready.sem, mean_ready.at(layer, b + 1))
                pool.tensor_tensor(rx[:, b:b + 1], mean, neg_half[:, 0:1], ALU.pow).then_inc(rx_ready.sem, 1)

            def settle_setup(ins):
                setup[0] += 1
                ins.then_inc(pool_setup, 1)
                pool.wait_ge(pool_setup, setup[0])

            def rotary_tables():
                pool.wait_ge(trig_ready, 1)
                for t, heads, half, at in ((0, IDX_HEADS, HD, 0), (2, HEADS, HS, HD)):
                    sin, cos = (trig[:, 4 + i, :].rearrange("p (b f) -> p b f", b=BLOCKS)[:, :, None, at:at + half]
                                .to_broadcast([P, BLOCKS, heads, half]) for i in range(2))
                    c, s = (tab[:, t + i, :].rearrange("p (b h d) -> p b h d", b=BLOCKS, h=heads) for i in range(2))
                    for part in range(2):
                        to = slice(part * half, (part + 1) * half)
                        settle_setup(pool.tensor_copy(c[:, :, :, to], cos))
                        settle_setup(pool.tensor_scalar(s[:, :, :, to], sin, (-1.0, 1.0)[part], None, ALU.mult))

            def rotary_angles():
                turn_parts = (6.28125, 0.0019350051879882812, 3.019916e-07)
                pi, magic = 3.1415925, 1.5 * 2.0 ** 23
                ang, whole, arg, product = trig[:, 0, :], trig[:, 1, :], trig[:, 2:4, :], trig[:, 6, :]
                pool.wait_ge(small_landed, 32)
                settle_setup(pool.tensor_copy(pos_f[:, :], pos_i[:, :]))
                for b in range(BLOCKS):
                    settle_setup(pool.tensor_scalar(ang[:, b * NF:(b + 1) * NF], frq[:, :], pos_f[:, b:b + 1], None, ALU.mult))
                settle_setup(pool.tensor_scalar(whole, ang, 1.0 / (2.0 * np.pi), magic, ALU.mult, ALU.add))
                settle_setup(pool.tensor_scalar(whole, whole, -magic, None, ALU.add))
                for part in turn_parts:
                    settle_setup(pool.tensor_scalar(product, whole, -part, None, ALU.mult))
                    settle_setup(pool.tensor_tensor(ang, ang, product, ALU.add))
                settle_setup(pool.tensor_copy(arg[:, 0, :], ang))
                settle_setup(pool.tensor_scalar(arg[:, 1, :], ang, 0.5 * np.pi, None, ALU.add))
                settle_setup(pool.tensor_scalar(whole, arg[:, 1, :], pi, -2.0 * np.pi, ALU.is_gt, ALU.mult))
                settle_setup(pool.tensor_tensor(arg[:, 1, :], arg[:, 1, :], whole, ALU.add))
                pool.tensor_scalar(arg, arg, pi, -pi, ALU.min, ALU.max).then_inc(angles_ready, 1)

            def body(layer):
                steps[0] = 0

                def link(ins):
                    steps[0] += 1
                    ins.then_inc(pool_chain.sem, 1)
                    pool.wait_ge(pool_chain.sem, pool_chain.at(layer, steps[0]))

                def inverse_root(dst, src, tmp, scale, eps, signal):
                    link(pool.tensor_scalar(tmp, src, scale, eps, ALU.mult, ALU.add))
                    pool.tensor_tensor(dst, tmp, neg_half[:, 0:dst.free_size()], ALU.pow).then_inc(signal.sem, 1)

                def split_lo(u):
                    pool.wait_ge(hi_done.sem, hi_done.at(layer, u + 1))
                    pool.tensor_tensor(unit(w_lo, u), unit(raw, u), unit(w_hi, u).bitcast(F32), ALU.subtract).then_inc(lo_done_pool.sem, 1)

                def rope(chunk, heads, half, table):
                    pool.wait_ge(proj_moved.sem, proj_moved.at(layer, place(layer, chunk, 1) + 1))
                    order = (IQ, DQ, DK, SQ, SK).index(chunk)
                    slot = order % 2
                    if order:
                        pool.wait_ge(rope_done.sem, rope_done.at(layer, order))
                    v = nat[:, slot, :, :].rearrange("p b (h d) -> p (b h) d", h=heads)
                    cos, sin, c, s = (a.rearrange("p (g d) -> p g d", d=2 * half)
                                      for a in (tab[:, table, :], tab[:, table + 1, :], rt[:, 0, :], rt[:, 1, :]))
                    link(pool.tensor_tensor(c, v[:, :, 0:2 * half], cos, ALU.mult))
                    link(pool.tensor_tensor(s[:, :, 0:half], v[:, :, half:2 * half], sin[:, :, 0:half], ALU.mult))
                    link(pool.tensor_tensor(s[:, :, half:2 * half], v[:, :, 0:half], sin[:, :, half:2 * half], ALU.mult))
                    pool.tensor_tensor(v[:, :, 0:2 * half], c, s, ALU.add).then_inc(rope_done.sem, 1)

                if layer:
                    split_lo(3)
                    root_x(layer, 1)
                else:
                    split_lo(3)
                pool.wait_ge(prm_landed.sem, prm_landed.at(layer, 16))
                link(pool.tensor_scalar(subln, subln, param("one_minus"), None, ALU.mult))
                for b in range(BLOCKS):
                    pool.wait_ge(proj_moved.sem, proj_moved.at(layer, place(layer, DG, b) + 1))
                    g = gate[:, b, 0, :].rearrange("p (h e) -> p h e", h=HEADS)
                    pool.tensor_tensor(g, g, subln[:, None, :].to_broadcast([P, HEADS, E]), ALU.mult).then_inc(gate_ready.sem, 1)
                for g in range(4, GROUPS + 1):
                    if g == 5 and layer == 0:
                        rotary_tables()
                    if g == 6:
                        rope(IQ, IDX_HEADS, HD, 0)
                    if g == 8:
                        pool.wait_ge(ik_var.sem, ik_var.at(layer, 1))
                        link(pool.tensor_scalar(ik_e, ik_mv[:, 1:4:2], LN_EPS, None, ALU.add))
                        pool.tensor_tensor(ik_r, ik_e, neg_half[:, 0:2], ALU.pow).then_inc(ik_rstd.sem, 1)
                    if g == 10:
                        rope(DQ, 2 * HEADS, HD, 0)
                    if g == 12:
                        rope(DK, 2 * HEADS, HD, 0)
                    if g == 14:
                        rope(SQ, HEADS, HS, 2)
                    if g == 16:
                        rope(SK, HEADS, HS, 2)
                    if g in (18, 19):
                        b = g - 18
                        pool.wait_ge(o_squared.sem, o_squared.at(layer, b + 1))
                        part = slice(HEADS * b, HEADS * (b + 1))
                        inverse_root(ro[:, part], ms_o[:, part], ep[:, 8 + 4 * b:12 + 4 * b], 1.0 / E, SUBLN_EPS, ro_ready)
                    if (g + 3) % RING == 3:
                        split_lo(g + 3)
                for b in range(BLOCKS):
                    pool.wait_ge(y_squared.sem, y_squared.at(layer, 2 * b + 2))
                    link(pool.tensor_tensor(ms_y[:, b:b + 1], ep[:, 2 * b:2 * b + 1], ep[:, 2 * b + 1:2 * b + 2], ALU.add))
                    inverse_root(ry[:, b:b + 1], ms_y[:, b:b + 1], ep[:, 6 + b:7 + b], 1.0 / D_MODEL, NORM_EPS, ry_ready)
                    if b == 0 and layer < DEPTH - 1:
                        root_x(layer + 1, 0)
                assert steps[0] == POOL_STEPS, steps[0]

            settle_setup(pool.memset(ident[:, :], 0.0))
            pool.affine_select(out=ident[:, :], in_=ident[:, :], compare_op=ALU.not_equal, fill=1.0,
                               base=0, pattern=[[-1, P]], channel_multiplier=1).then_inc(ident_ready, 1)
            settle_setup(pool.memset(neg_half, -0.5))
            pool.wait_ge(ident_ready, 1)
            settle_setup(pool.tensor_copy(ident_b[:, :], ident[:, :]))
            settle_setup(pool.memset(causal[:, :], 0.0))
            settle_setup(pool.affine_select(out=causal[:, P:SEQ], in_=causal[:, P:SEQ], compare_op=ALU.is_ge, fill=NEG,
                                            base=0, pattern=[[-1, P]], channel_multiplier=1))
            pool.tensor_copy(causal_b[:, :], causal[:, :]).then_inc(masks_ready, 1)
            rotary_angles()
            root_x(0, 0)
            root_x(0, 1)
            for layer in range(DEPTH):
                body(layer)


DVE_STEPS = 86
POOL_STEPS = 23


def kernel(x, positions, pre_norm_w, post_norm_w, w_in, w_out, lambda_q1, lambda_k1, lambda_q2, lambda_k2,
           diff_subln_w, idx_k_norm_w, idx_k_norm_b):
    import math

    import concourse.bacc as bacc
    from concourse.bass_utils import run_bass_kernel_spmd

    freqs = np.concatenate([np.float32(ROPE_THETA) ** (-np.arange(0, 2 * n, 2, dtype=np.float32) / np.float32(2 * n))
                            for n in (HD, HS)]).astype(np.float32)[None, :]
    init = [0.8 - 0.6 * math.exp(-0.3 * layer) for layer in range(DEPTH)]
    consts = np.array([[v, 1.0 - v] for v in init], np.float32)
    f = np.ascontiguousarray
    arrays = {
        "x": f(x), "positions": f(np.asarray(positions).reshape(BLOCKS, P).T), "freqs": freqs,
        "pre_t": f(np.asarray(pre_norm_w).reshape(DEPTH * KT, P).T),
        "rows": f(np.concatenate([np.asarray(a) for a in (lambda_q1, lambda_k1, lambda_q2, lambda_k2, diff_subln_w,
                                                          idx_k_norm_w, idx_k_norm_b, post_norm_w)] + [consts], axis=1)),
        "w_in": f(w_in), "w_out": f(w_out),
    }
    nc = bacc.Bacc("TRN2", target_bir_lowering=False, num_devices=1)
    args = [nc.dram_tensor(f"in_{name}", a.shape, mybir.dt.from_np(a.dtype), kind="ExternalInput").ap() for name, a in arrays.items()]
    result = nc.dram_tensor("out", (1, SEQ, D_MODEL), F32, kind="ExternalOutput").ap()
    build_trunk(nc, *args, result)
    r = run_bass_kernel_spmd(nc, [{f"in_{name}": a for name, a in arrays.items()}], core_ids=[0])
    return r.results[0]["out"]
```

```python
from contextlib import ExitStack

import numpy as np

import concourse.bass as bass
from concourse import mybir

F32 = mybir.dt.float32
F32R = mybir.dt.float32r
I32 = mybir.dt.int32
ALU = mybir.AluOpType
ACT = mybir.ActivationFunctionType
AX = mybir.AxisListType

P = 128
DEPTH = 2
SEQ = 256
D_MODEL = 1024
WIDTH = 512
HEADS = 4
E = WIDTH // HEADS
DIFF_QK = E // 2
IDX_HEADS = 8
IDX_DIM = WIDTH // IDX_HEADS
N_IN = 9 * WIDTH + IDX_DIM + IDX_HEADS
TOPK = min(256, SEQ // 4)
ROPE_THETA = 500000.0
ROPE_FRACTION = 4
NORM_EPS, SUBLN_EPS, LN_EPS = 1e-6, 1e-5, 1e-6

BLOCKS = SEQ // P
KT = D_MODEL // P
FIRST_TILES = 2
WARM_UP = 6
HALF = KT // 2
NEG = -1e30
TAKEN = -3e38
TAKEN_ABOVE = -2e38

DG, SG, IQ, TAIL, DQ, DK, SQ, SK, DV, SV = range(10)
COLUMNS = [(3, WIDTH), (7, WIDTH), (8, WIDTH), (9, IDX_DIM + IDX_HEADS), (0, WIDTH), (1, WIDTH),
           (4, WIDTH), (5, WIDTH), (2, WIDTH), (6, WIDTH)]
CHUNKS = len(COLUMNS)
IN_UNITS = 2 * CHUNKS
UNITS = IN_UNITS + 4
GROUPS = BLOCKS * CHUNKS
RING = 4
assert UNITS % RING == 0
TAIL_GROUP, TAIL_BACK = BLOCKS * TAIL, BLOCKS * TAIL + 1
TAIL_N = COLUMNS[TAIL][1]
REST = [(c, b) for c in range(2, CHUNKS) for b in range(BLOCKS)]


def order(layer):
    return ([(0, 0), (0, 1), (1, 0), (1, 1)] if layer == 0 else [(0, 0), (1, 0), (0, 1), (1, 1)]) + REST


def place(layer, chunk, b):
    return order(layer).index((chunk, b))


HD = DIFF_QK // ROPE_FRACTION // 2
HS = E // ROPE_FRACTION // 2
NF = HD + HS

ROW = dict(lq1=DIFF_QK, lk1=DIFF_QK, lq2=DIFF_QK, lk2=DIFF_QK, subln=E, ik_w=IDX_DIM, ik_b=IDX_DIM,
           post=D_MODEL, lam_init=1, one_minus=1)
AT = {}
for _name, _n in ROW.items():
    AT[_name] = (sum(ROW[x] for x in AT), sum(ROW[x] for x in AT) + _n)
ROW_N = sum(ROW.values())

T_IQ, T_IK, T_DQ, T_DK, T_SQ, T_PD0, T_PD1A = 4, 6, 7, 9, 11, 13, 14
T_SK, T_PD1B, T_MD0, T_PS0, T_MD1, T_PS1A, T_PS1B, T_MS0, T_MS1 = 15, 17, 18, 19, 20, 21, 22, 23, 24
T_USES = 25
S_DIFF0, S_USES = 6, 15


class Count:

    def __init__(self, sem, per_layer, before=0):
        self.sem, self.per_layer, self.before = sem, per_layer, before

    def at(self, layer, n):
        return layer * self.per_layer + (self.before + n)


def build_trunk(nc, x, positions, freqs, pre_t, rows, w_in, w_out, out):
    ctx = ExitStack()
    with ctx:
        def sb(name, shape, dt=F32):
            return ctx.enter_context(nc.sbuf_tensor(name, shape, dt))

        def pb(name, shape, dt=F32):
            return ctx.enter_context(nc.psum_tensor(name, shape, dt))

        def sem(name):
            return ctx.enter_context(nc.semaphore(name))

        def count(name, per_layer, before=0):
            return Count(sem(name), per_layer, before)

        raw = sb("w_raw", [P, RING, HALF, WIDTH])
        w_hi = sb("w_hi", [P, RING, HALF, WIDTH], F32R)
        w_lo = sb("w_lo", [P, RING, HALF, WIDTH], F32R)
        h_hi = sb("h_hi", [P, KT, SEQ], F32R)
        h_lo = sb("h_lo", [P, KT, SEQ], F32R)
        m_hi = sb("m_hi", [P, HALF, SEQ], F32R)
        m_lo = sb("m_lo", [P, HALF, SEQ], F32R)
        xres = sb("xres", [P, BLOCKS, D_MODEL])
        gate = sb("gate", [P, BLOCKS, 2, WIDTH])
        nat = sb("nat", [P, 2, BLOCKS, WIDTH])
        v_diff = sb("v_diff", [P, BLOCKS, WIDTH])
        v_dsa = sb("v_dsa", [P, BLOCKS, WIDTH])
        ikn = sb("ikn", [P, BLOCKS, IDX_DIM + IDX_HEADS])
        ik2 = sb("ik2", [P, BLOCKS, 2, IDX_DIM])
        iqT = sb("iqT", [P, HEADS, SEQ])
        ikT = sb("ikT", [P, SEQ])
        dqT = sb("dqT", [P, HEADS, SEQ])
        dkT = sb("dkT", [P, HEADS, SEQ])
        sqT = sb("sqT", [P, HEADS, SEQ])
        skT = iqT
        pbuf = sb("pbuf", [P, 4, WIDTH])
        pT = sb("pT", [P, 3, WIDTH])
        mixn = sb("mixn", [P, 2, WIDTH])
        work = [sb("work0", [P, P]), sb("work1", [P, SEQ])]
        top8 = sb("top8", [P, 8])
        prm = sb("prm", [P, ROW_N])
        preT = sb("preT", [P, DEPTH, KT])
        tab = sb("tab", [P, 4, SEQ])
        rt = sb("rt", [P, 2, SEQ])
        trig = sb("trig", [P, 8, BLOCKS * NF])
        frq = sb("frq", [P, NF])
        pos_i = sb("pos_i", [P, BLOCKS], I32)
        pos_f = sb("pos_f", [P, BLOCKS])
        ident = sb("ident", [P, P])
        causal = sb("causal", [P, SEQ])
        st = sb("st", [P, 160])
        neg_half = st[:, 0:8]
        ms_x, rx, ry = st[:, 8:10], st[:, 10:12], st[:, 14:16]
        ms_o, ro = st[:, 16:24], st[:, 24:32]
        ep = st[:, 32:48]
        lam_s, lam_e, neg_lam = st[:, 48:50], st[:, 50:52], st[:, 52:53]
        ik_st, ik_mv, ik_r, ik_e = st[:, 56:68], st[:, 68:72], st[:, 72:74], st[:, 74:76]
        spare = st[:, 76:77]
        iw = st[:, 80:96]
        neg_max = st[:, 96:112]
        sums = st[:, 112:128]
        inv = st[:, 128:144]

        A = [pb("bank_a0", [P, WIDTH]), pb("bank_a1", [P, WIDTH])]
        S = [pb("bank_s0", [P, WIDTH]), pb("bank_s1", [P, WIDTH])]
        T = [pb("bank_t0", [P, WIDTH]), pb("bank_t1", [P, WIDTH])]
        O = [pb("bank_o0", [P, WIDTH]), pb("bank_o1", [P, WIDTH])]
        Y = [[A[1], A[0]], S]

        raw_landed = [count(f"raw_landed{i}", 16 * (UNITS // RING)) for i in range(RING)]
        hi_done = count("hi_done", UNITS)
        lo_done_dve = count("lo_done_dve", UNITS // RING * 3)
        lo_done_pool = count("lo_done_pool", UNITS // RING)
        first_piece = [sem("first_piece_landed"), sem("first_piece_hi")]
        first_half_used = count("first_half_used", CHUNKS)
        out_unit_used = count("out_unit_used", 3, 1)
        proj_done = count("proj_done", GROUPS)
        proj_moved = count("proj_moved", GROUPS)
        y_done = count("y_done", 2, 1)
        y_read = count("y_read", 2, 2)
        x_landed = [sem(f"x_landed{b}") for b in range(BLOCKS)]
        small_landed = sem("small_landed")
        pre_landed = sem("pre_landed")
        prm_landed = count("prm_landed", 16)
        x_ready = count("x_ready", 2 * BLOCKS)
        out_landed = sem("out_landed")
        t_filled = count("t_filled", T_USES)
        t_drained = count("t_drained", T_USES, 1)
        s_filled = count("s_filled", S_USES)
        s_freed = count("s_freed", S_USES)
        exps_done = count("exps_done", S_USES - S_DIFF0)
        idx_used = count("idx_used", S_DIFF0)
        o_filled = count("o_filled", 4)
        o_squared = count("o_squared", 2)
        x_squared = count("x_squared", 2)
        y_squared = count("y_squared", 2 * BLOCKS)
        mean_ready = count("mean_ready", 2)
        rx_ready = count("rx_ready", 2)
        ry_ready = count("ry_ready", 2)
        ro_ready = count("ro_ready", 2)
        ik_var = count("ik_var", 1)
        ik_rstd = count("ik_rstd", 1)
        ik_ready = count("ik_ready", 1)
        h_hi_done = count("h_hi_done", 4)
        h_lo_done = count("h_lo_done", 4)
        rope_done = count("rope_done", 5)
        gate_ready = count("gate_ready", 2)
        combined = count("combined", 3)
        mixn_ready = count("mixn_ready", 4, 2)
        lam_summed = count("lam_summed", 1)
        lam_exped = count("lam_exped", 1)
        ident_ready = sem("ident_ready")
        neg_half_ready = sem("neg_half_ready")
        causal_ready = sem("causal_ready")
        angles_ready = sem("angles_ready")
        trig_ready = sem("trig_ready")
        pool_chain = count("pool_chain", POOL_STEPS)
        dve_chain = count("dve_chain", DVE_STEPS)
        pool_setup = sem("pool_setup")

        def chunk_width(u):
            return COLUMNS[u // 2][1] if u < IN_UNITS else WIDTH

        def unit(ring, u):
            return ring[:, u % RING, :, 0:chunk_width(u)]

        def lo_of(u):
            return (lo_done_pool, u // RING + 1) if u % RING == 3 else (lo_done_dve, 3 * (u // RING) + u % RING + 1)

        def weights(layer, u):
            if u < IN_UNITS:
                part, width = COLUMNS[u // 2]
                k0, c0, w = u % 2 * HALF * P, part * WIDTH, w_in
            else:
                width = WIDTH
                k0, c0, w = (u - IN_UNITS) // 2 * HALF * P, (u - IN_UNITS) % 2 * WIDTH, w_out
            return w[layer, k0:k0 + HALF * P, c0:c0 + width].rearrange("(k p) n -> p k n", p=P)

        def param(name):
            a, b = AT[name]
            return prm[:, a:b]

        def bank_of(g):
            return A[(g if g < TAIL_BACK else g - 1) % 2]

        subln = param("subln")
        y_w = pbuf[:, :, :].rearrange("p (b a) n -> p b (a n)", b=BLOCKS)
        tail_t = pbuf[0:TAIL_N, 2, 0:SEQ]
        ik_tmp = pbuf[:, 1, 0:2 * BLOCKS * 2 * HD].rearrange("p (t b d) -> p t b d", t=2, b=BLOCKS)
        block = ctx.enter_context(nc.Block())

        @block.sync
        def _(sp):
            sp.dma_start(xres[:, 0, :], x[0, 0:P, :]).then_inc(x_landed[0], 16)
            sp.dma_start(raw[:, 0, 0:FIRST_TILES, :], weights(0, 0)[:, 0:FIRST_TILES, :]).then_inc(first_piece[0], 16)
            sp.dma_start(raw[:, 0, FIRST_TILES:HALF, :], weights(0, 0)[:, FIRST_TILES:HALF, :]).then_inc(raw_landed[0].sem, 16)
            sp.dma_start(xres[:, 1, :], x[0, P:SEQ, :]).then_inc(x_landed[1], 16)
            for u in range(1, RING):
                sp.dma_start(unit(raw, u), weights(0, u)).then_inc(raw_landed[u].sem, 16)
            sp.dma_start(prm[:, :], rows[0:1, :].to_broadcast([P, ROW_N])).then_inc(prm_landed.sem, 16)
            for layer in range(DEPTH):
                for u in range(UNITS - RING):
                    done, n = lo_of(u)
                    sp.wait_ge(done.sem, done.at(layer, n))
                    sp.dma_start(unit(raw, u + RING), weights(layer, u + RING)).then_inc(raw_landed[u % RING].sem, 16)
                if layer < DEPTH - 1:
                    for u in range(RING):
                        done, n = lo_of(UNITS - RING + u)
                        sp.wait_ge(done.sem, done.at(layer, n))
                        sp.dma_start(unit(raw, u), weights(layer + 1, u)).then_inc(raw_landed[u].sem, 16)
                    sp.wait_ge(y_read.sem, y_read.at(layer, 2))
                    sp.dma_start(prm[:, :], rows[layer + 1:layer + 2, :].to_broadcast([P, ROW_N])).then_inc(prm_landed.sem, 16)
            for b in range(BLOCKS):
                for n in range(2):
                    part = slice(n * WIDTH, (n + 1) * WIDTH)
                    sp.wait_ge(x_ready.sem, x_ready.at(DEPTH, 2 * b + n + 1))
                    sp.dma_start(out[0, b * P:(b + 1) * P, part], xres[:, b, part]).then_inc(out_landed, 16)
            sp.wait_ge(out_landed, 16 * 2 * BLOCKS)

        @block.tensor
        def _(pe):
            def turn_x(layer, b):
                for n in range(2):
                    pe.wait_ge(x_ready.sem, x_ready.at(layer, 2 * b + n + 1))
                    pe.wait_ge(t_drained.sem, t_drained.at(layer, max(2 * b + n - 1, 0)))
                    for k in range(HALF):
                        at = (HALF * n + k) * P
                        mm = pe.transpose(T[n][:, k * P:(k + 1) * P], xres[:, b, at:at + P], ident[:, :])
                    mm.then_inc(t_filled.sem, 1)

            def body(layer):
                def bank_t(j):
                    pe.wait_ge(t_drained.sem, t_drained.at(layer, j - 1))
                    return T[j % 2]

                def bank_s(j):
                    if j < 2:
                        pe.wait_ge(y_read.sem, y_read.at(layer, 0))
                    else:
                        pe.wait_ge(s_freed.sem, s_freed.at(layer, j - 1))
                    return S[j % 2]

                def turn(j, parts):
                    bank = bank_t(j)
                    for n, part in enumerate(parts):
                        mm = pe.transpose(bank[:, n * P:(n + 1) * P], part, ident[:, :])
                    mm.then_inc(t_filled.sem, 1)

                def turn_nat(j, slot, rope):
                    pe.wait_ge(rope_done.sem, rope_done.at(layer, rope))
                    for n in range(2):
                        turn(j + n, [nat[:, slot, b, f * P:(f + 1) * P] for f in (2 * n, 2 * n + 1) for b in range(BLOCKS)])

                def part_of(g, half):
                    chunk, b = order(layer)[g]
                    u, width, tok = 2 * chunk + half, COLUMNS[chunk][1], slice(b * P, (b + 1) * P)
                    bank = bank_of(g)[:, 0:width]
                    whi, wlo = unit(w_hi, u), unit(w_lo, u)
                    pe.wait_ge(h_hi_done.sem, h_hi_done.at(layer, 2 * b + half + 1))
                    if layer == 0 and g == 0 and half == 0:
                        pe.wait_ge(first_piece[1], 1)
                    else:
                        pe.wait_ge(hi_done.sem, hi_done.at(layer, u + 1))
                    for kk in range(HALF):
                        if layer == 0 and g == 0 and half == 0 and kk == FIRST_TILES:
                            pe.wait_ge(hi_done.sem, 1)
                        pe.matmul(bank, h_hi[:, HALF * half + kk, tok], whi[:, kk, :], start=half == 0 and kk == 0, stop=False)
                    if layer == 0 and g == 0 and half == 0:
                        turn_x(layer, 1)
                    pe.wait_ge(h_lo_done.sem, h_lo_done.at(layer, 2 * b + half + 1))
                    for kk in range(HALF):
                        pe.matmul(bank, h_lo[:, HALF * half + kk, tok], whi[:, kk, :], start=False, stop=False)
                    done, n = lo_of(u)
                    pe.wait_ge(done.sem, done.at(layer, n))
                    for kk in range(HALF):
                        mm = pe.matmul(bank, h_hi[:, HALF * half + kk, tok], wlo[:, kk, :], start=False,
                                       stop=half == 1 and kk == HALF - 1)
                    return mm

                def first(g):
                    if g < 2:
                        pe.wait_ge(y_read.sem, y_read.at(layer, -1))
                    else:
                        pe.wait_ge(proj_moved.sem, proj_moved.at(layer, g - 2 if g == TAIL_BACK + 1 else g - 1))
                    mm = part_of(g, 0)
                    if order(layer)[g][1] == 1:
                        mm.then_inc(first_half_used.sem, 1)

                def second(g):
                    part_of(g, 1).then_inc(proj_done.sem, 1)

                def tail_products():
                    bank = bank_of(TAIL_GROUP)[0:TAIL_N, 0:SEQ]
                    pe.wait_ge(proj_moved.sem, proj_moved.at(layer, TAIL_GROUP - 1))
                    for half in range(2):
                        u = 2 * TAIL + half
                        done, n = lo_of(u)
                        pe.wait_ge(done.sem, done.at(layer, n))
                        for i, (w, x) in enumerate(((w_hi, h_hi), (w_hi, h_lo), (w_lo, h_hi))):
                            for kk in range(HALF):
                                mm = pe.matmul(bank, unit(w, u)[:, kk, :], x[:, HALF * half + kk, :],
                                               start=half == 0 and i == 0 and kk == 0,
                                               stop=half == 1 and i == 2 and kk == HALF - 1)
                        mm.then_inc((first_half_used if half == 0 else proj_done).sem, 1)

                def tail_back():
                    pe.wait_ge(proj_moved.sem, proj_moved.at(layer, TAIL_GROUP + 1))
                    for b in range(BLOCKS):
                        mm = pe.transpose(bank_of(TAIL_BACK)[:, b * TAIL_N:(b + 1) * TAIL_N],
                                          tail_t[:, b * P:(b + 1) * P], ident[0:TAIL_N, 0:TAIL_N])
                    mm.then_inc(proj_done.sem, 1)

                def index_logits(j, b, pairs):
                    banks, n = (bank_s(j), bank_s(j + 1)), P * (b + 1)
                    for i, pair in enumerate(pairs):
                        for odd in range(2):
                            rows_h = slice(IDX_DIM * odd, IDX_DIM * (odd + 1))
                            mm = pe.matmul(banks[odd][:, i * n:(i + 1) * n], iqT[rows_h, pair, b * P:(b + 1) * P],
                                           ikT[rows_h, 0:n], start=True, stop=True)
                            if i == len(pairs) - 1:
                                mm.then_inc(s_filled.sem, 1)

                def diff_scores(j, b, heads):
                    banks, n = (bank_s(j), bank_s(j + 1)), P * (b + 1)
                    for i, h in enumerate(heads):
                        for m in range(2):
                            rows_m = slice(DIFF_QK * m, DIFF_QK * (m + 1))
                            mm = pe.matmul(banks[m][:, i * n:(i + 1) * n], dqT[rows_m, h, b * P:(b + 1) * P],
                                           dkT[rows_m, h, 0:n], start=True, stop=True)
                            if i == len(heads) - 1:
                                mm.then_inc(s_filled.sem, 1)

                def dsa_scores(j, b, heads):
                    bank, n = bank_s(j), P * (b + 1)
                    for i, h in enumerate(heads):
                        mm = pe.matmul(bank[:, i * n:(i + 1) * n], sqT[:, h, b * P:(b + 1) * P],
                                       skT[:, h, 0:n], start=True, stop=True)
                    mm.then_inc(s_filled.sem, 1)

                def turn_probs(j, use, b, heads):
                    n = P * (b + 1)
                    turn(j, [pbuf[:, use % 4, i * n + t * P:i * n + (t + 1) * P] for i in range(heads) for t in range(b + 1)])

                def values(o, b, v, tiles, drained, moved):
                    pe.wait_ge(t_drained.sem, t_drained.at(layer, drained))
                    pe.wait_ge(proj_moved.sem, proj_moved.at(layer, moved))
                    pe.wait_ge(mixn_ready.sem, mixn_ready.at(layer, o - 1))
                    for h, parts in enumerate(tiles):
                        for t, part in enumerate(parts):
                            mm = pe.matmul(O[o % 2][:, h * E:(h + 1) * E], part, v[:, t, h * E:(h + 1) * E],
                                           start=(t == 0), stop=(t == len(parts) - 1))
                    mm.then_inc(o_filled.sem, 1)

                def slot(i, n):
                    return pT[:, i, n * P:(n + 1) * P]

                def turn_mix(j, i, o):
                    pe.wait_ge(mixn_ready.sem, mixn_ready.at(layer, o + 1))
                    turn(j, [mixn[:, i, k * P:(k + 1) * P] for k in range(HALF)])

                def out_part(half, b, n):
                    x_hi, x_lo = (m_hi, m_lo) if half == 0 else (h_hi, h_lo)
                    u, tok = IN_UNITS + 2 * half + n, slice(b * P, (b + 1) * P)
                    bank = Y[b][n][:, :]
                    done, at = lo_of(u)
                    pe.wait_ge(done.sem, done.at(layer, at))
                    for i, (x, w) in enumerate(((x_hi, w_hi), (x_lo, w_hi), (x_hi, w_lo))):
                        for kk in range(HALF):
                            mm = pe.matmul(bank, x[:, kk, tok], w[:, u % RING, kk, :], start=half == 0 and i == 0 and kk == 0,
                                           stop=half == 1 and i == 2 and kk == HALF - 1)
                    return mm

                if layer == 0:
                    first(0)
                    first(1)
                    second(0)
                    second(1)
                else:
                    first(0)
                    second(0)
                    first(1)
                    turn_x(layer, 1)
                    second(1)
                for g in range(2, TAIL_GROUP):
                    first(g)
                    second(g)
                tail_products()
                first(8)
                tail_back()
                second(8)
                turn_nat(T_IQ, 0, 1)
                first(9)
                second(9)
                pe.wait_ge(ik_ready.sem, ik_ready.at(layer, 1))
                turn(T_IK, [ik2[:, b, :, :].rearrange("p t d -> p (t d)") for b in range(BLOCKS)])
                first(10)
                pe.wait_ge(t_drained.sem, t_drained.at(layer, T_IK + 1))
                index_logits(0, 0, range(4))
                second(10)
                index_logits(2, 1, (0, 1))
                first(11)
                turn_nat(T_DQ, 1, 2)
                index_logits(4, 1, (2, 3))
                second(11)
                first(12)
                second(12)
                turn_nat(T_DK, 0, 3)
                first(13)
                pe.wait_ge(t_drained.sem, t_drained.at(layer, T_DK + 2))
                diff_scores(6, 0, range(HEADS))
                second(13)
                first(14)
                diff_scores(8, 1, (0, 1))
                second(14)
                turn_nat(T_SQ, 1, 4)
                first(15)
                pe.wait_ge(combined.sem, combined.at(layer, 1))
                turn_probs(T_PD0, 6, 0, HEADS)
                diff_scores(10, 1, (2, 3))
                second(15)
                pe.wait_ge(combined.sem, combined.at(layer, 2))
                turn_probs(T_PD1A, 8, 1, 2)
                first(16)
                second(16)
                turn_nat(T_SK, 0, 5)
                first(17)
                pe.wait_ge(combined.sem, combined.at(layer, 3))
                turn_probs(T_PD1B, 10, 1, 2)
                pe.wait_ge(t_drained.sem, t_drained.at(layer, T_SK + 2))
                dsa_scores(12, 0, range(HEADS))
                values(0, 0, v_diff, [[slot(0, h)] for h in range(HEADS)], T_PD0 + 1, place(layer, DV, 0) + 1)
                second(17)
                first(18)
                dsa_scores(13, 1, (0, 1))
                dsa_scores(14, 1, (2, 3))
                values(1, 1, v_diff, [[slot(1 + h // 2, 2 * (h % 2) + t) for t in range(2)] for h in range(HEADS)],
                       T_PD1B + 1, place(layer, DV, 1) + 1)
                second(18)
                turn_mix(T_MD0, 0, 0)
                first(19)
                pe.wait_ge(exps_done.sem, exps_done.at(layer, 13 - S_DIFF0))
                turn_probs(T_PS0, 12, 0, HEADS)
                second(19)
                turn_mix(T_MD1, 1, 1)
                values(2, 0, v_dsa, [[slot(0, h)] for h in range(HEADS)], T_PS0 + 1, place(layer, SV, 0) + 1)
                pe.wait_ge(exps_done.sem, exps_done.at(layer, 15 - S_DIFF0))
                turn_probs(T_PS1A, 13, 1, 2)
                pe.wait_ge(t_drained.sem, t_drained.at(layer, T_MD0 + 1))
                out_part(0, 0, 0)
                turn_probs(T_PS1B, 14, 1, 2)
                turn_mix(T_MS0, 0, 2)
                pe.wait_ge(proj_moved.sem, proj_moved.at(layer, GROUPS))
                out_part(0, 0, 1)
                values(3, 1, v_dsa, [[slot(1 + h // 2, 2 * (h % 2) + t) for t in range(2)] for h in range(HEADS)],
                       T_PS1B + 1, place(layer, SV, 1) + 1)
                pe.wait_ge(t_drained.sem, t_drained.at(layer, T_MS0 + 1))
                out_part(1, 0, 0)
                out_part(1, 0, 1).then_inc(y_done.sem, 1)
                pe.wait_ge(t_drained.sem, t_drained.at(layer, T_MD1 + 1))
                out_part(0, 1, 0).then_inc(out_unit_used.sem, 1)
                turn_mix(T_MS1, 1, 3)
                out_part(0, 1, 1).then_inc(out_unit_used.sem, 1)
                pe.wait_ge(t_drained.sem, t_drained.at(layer, T_MS1 + 1))
                out_part(1, 1, 0).then_inc(out_unit_used.sem, 1)
                if layer < DEPTH - 1:
                    turn_x(layer + 1, 0)
                out_part(1, 1, 1).then_inc(y_done.sem, 1)

            pe.wait_ge(ident_ready, 1)
            for _ in range(WARM_UP):
                pe.matmul(O[0][:, 0:P], ident[:, :], ident[:, :], start=True, stop=True)
            turn_x(0, 0)
            for _ in range(WARM_UP):
                pe.matmul(O[0][:, 0:P], ident[:, :], ident[:, :], start=True, stop=True)
            for layer in range(DEPTH):
                body(layer)

        @block.scalar
        def _(act):
            def split_hi(layer, u):
                if u >= RING:
                    v = u - RING
                    if v % 2 == 0:
                        act.wait_ge(first_half_used.sem, first_half_used.at(layer, v // 2 + 1))
                    else:
                        last = TAIL_GROUP if v // 2 == TAIL else place(layer, v // 2, 1)
                        act.wait_ge(proj_done.sem, proj_done.at(layer, last + 1))
                act.wait_ge(raw_landed[u % RING].sem, raw_landed[u % RING].at(layer, 16 * (u // RING + 1)))
                act.activation(unit(w_hi, u), unit(raw, u), ACT.Copy).then_inc(hi_done.sem, 1)

            def x_hi(layer, b):
                for n in range(2):
                    j = 2 * b + n
                    act.wait_ge(t_drained.sem, t_drained.at(layer, j + 1))
                    act.activation(h_hi[:, HALF * n:HALF * (n + 1), b * P:(b + 1) * P],
                                   pT[:, j % 3, :].rearrange("p (k t) -> p k t", k=HALF), ACT.Copy).then_inc(h_hi_done.sem, 1)

            def square_x(layer, b):
                act.wait_ge(x_ready.sem, x_ready.at(layer, 2 * b + 2))
                act.activation(nat[:, b, :, :].rearrange("p a n -> p (a n)"), xres[:, b, :], ACT.Square,
                               accum_out=ms_x[:, b:b + 1]).then_inc(x_squared.sem, 1)

            def body(layer):
                def move(g):
                    chunk, b = order(layer)[g]
                    width = COLUMNS[chunk][1]
                    act.wait_ge(proj_done.sem, proj_done.at(layer, g + 1))
                    if g == TAIL_GROUP:
                        act.activation(tail_t, bank_of(g)[0:TAIL_N, 0:SEQ], ACT.Copy).then_inc(proj_moved.sem, 1)
                        return
                    if g == TAIL_BACK:
                        for b in range(BLOCKS):
                            ins = act.activation(ikn[:, b, :], bank_of(g)[:, b * TAIL_N:(b + 1) * TAIL_N], ACT.Copy,
                                                 scale=rx[:, b:b + 1])
                        ins.then_inc(proj_moved.sem, 1)
                        return
                    dst = {DG: gate[:, b, 0, :], SG: gate[:, b, 1, :], DV: v_diff[:, b, :],
                           SV: v_dsa[:, b, :], IQ: nat[:, 0, b, :], DQ: nat[:, 1, b, :], DK: nat[:, 0, b, :],
                           SQ: nat[:, 1, b, :], SK: nat[:, 0, b, :]}[chunk]
                    if g == place(layer, 0, b):
                        act.wait_ge(rx_ready.sem, rx_ready.at(layer, b + 1))
                    act.activation(dst, bank_of(g)[:, 0:width], ACT.Silu if chunk in (DG, SG) else ACT.Copy,
                                   scale=rx[:, b:b + 1]).then_inc(proj_moved.sem, 1)

                def relu(j):
                    act.wait_ge(s_filled.sem, s_filled.at(layer, j + 1))
                    if j >= 4:
                        act.wait_ge(idx_used.sem, idx_used.at(layer, j - 3))
                    act.activation(pbuf[:, j % 4, :], S[j % 2][:, :], ACT.Relu).then_inc(s_freed.sem, 1)

                def exps(j, b, n_rows):
                    n, r = P * (b + 1), 4 * (j % 4)
                    act.wait_ge(s_freed.sem, s_freed.at(layer, j + 1))
                    for i in range(n_rows):
                        terms = pbuf[:, j % 4, i * n:(i + 1) * n]
                        ins = act.activation(terms, terms, ACT.Exp, scale=-1.0,
                                             bias=neg_max[:, r + i:r + i + 1], accum_out=sums[:, r + i:r + i + 1])
                    ins.then_inc(exps_done.sem, 1)

                def square_o(b):
                    act.wait_ge(o_filled.sem, o_filled.at(layer, b + 1))
                    for h in range(HEADS):
                        ins = act.activation(mixn[:, b, h * E:(h + 1) * E], O[b][:, h * E:(h + 1) * E], ACT.Square,
                                             accum_out=ms_o[:, HEADS * b + h:HEADS * b + h + 1])
                    ins.then_inc(o_squared.sem, 1)

                def square_y(b):
                    bank = Y[b]
                    for n in range(2):
                        if (b, n) == (1, 0):
                            act.wait_ge(out_unit_used.sem, out_unit_used.at(layer, 3))
                        else:
                            act.wait_ge(y_done.sem, y_done.at(layer, b + 1))
                        act.activation(nat[:, b, n, :], bank[n][:, :], ACT.Square,
                                       accum_out=ep[:, 2 * b + n:2 * b + n + 1]).then_inc(y_squared.sem, 1)

                act.wait_ge(y_done.sem, y_done.at(layer, 0))
                split_hi(layer, 3)
                if layer:
                    square_x(layer, 1)
                move(0)
                if layer:
                    x_hi(layer, 1)
                move(1)
                split_hi(layer, 4)
                if layer == 0:
                    split_hi(layer, 5)
                move(2)
                if layer:
                    split_hi(layer, 5)
                split_hi(layer, 6)
                move(3)
                split_hi(layer, 7)
                if layer == 0:
                    act.wait_ge(angles_ready, 1)
                    act.activation(trig[:, 4:6, :], trig[:, 2:4, :], ACT.Sin).then_inc(trig_ready, 1)
                for g in range(5, 10):
                    move(g - 1)
                    split_hi(layer, g + 3)
                move(9)
                split_hi(layer, 13)
                relu(0)
                relu(1)
                move(10)
                relu(2)
                relu(3)
                split_hi(layer, 14)
                relu(4)
                relu(5)
                move(11)
                act.wait_ge(lam_summed.sem, lam_summed.at(layer, 1))
                act.activation(lam_e, lam_s, ACT.Exp).then_inc(lam_exped.sem, 1)
                split_hi(layer, 15)
                move(12)
                split_hi(layer, 16)
                exps(6, 0, 4)
                exps(7, 0, 4)
                move(13)
                split_hi(layer, 17)
                exps(8, 1, 2)
                exps(9, 1, 2)
                move(14)
                split_hi(layer, 18)
                exps(10, 1, 2)
                exps(11, 1, 2)
                move(15)
                split_hi(layer, 19)
                move(16)
                split_hi(layer, 20)
                exps(12, 0, 4)
                move(17)
                square_o(0)
                split_hi(layer, 21)
                exps(13, 1, 2)
                exps(14, 1, 2)
                square_o(1)
                move(18)
                split_hi(layer, 22)
                move(19)
                split_hi(layer, 23)
                square_y(0)
                if layer < DEPTH - 1:
                    act.wait_ge(out_unit_used.sem, out_unit_used.at(layer, 1))
                    split_hi(layer + 1, 0)
                    act.wait_ge(out_unit_used.sem, out_unit_used.at(layer, 2))
                    split_hi(layer + 1, 1)
                    act.wait_ge(out_unit_used.sem, out_unit_used.at(layer, 3))
                    split_hi(layer + 1, 2)
                    x_hi(layer + 1, 0)
                    square_x(layer + 1, 0)
                square_y(1)

            act.dma_start(preT[:, :, :], pre_t.rearrange("p (l k) -> p l k", l=DEPTH)).then_inc(pre_landed, 16)
            act.dma_start(pos_i[:, :], positions).then_inc(small_landed, 16)
            act.dma_start(frq[:, :], freqs.to_broadcast([P, NF])).then_inc(small_landed, 16)
            act.wait_ge(neg_half_ready, 1)
            act.activation(spare, neg_half[:, 0:1], ACT.Silu)
            act.wait_ge(first_piece[0], 16)
            act.activation(w_hi[:, 0, 0:FIRST_TILES, :], raw[:, 0, 0:FIRST_TILES, :], ACT.Copy).then_inc(first_piece[1], 1)
            x_hi(0, 0)
            act.wait_ge(raw_landed[0].sem, 16)
            act.activation(w_hi[:, 0, FIRST_TILES:HALF, :], raw[:, 0, FIRST_TILES:HALF, :], ACT.Copy).then_inc(hi_done.sem, 1)
            square_x(0, 0)
            x_hi(0, 1)
            split_hi(0, 1)
            square_x(0, 1)
            split_hi(0, 2)
            for layer in range(DEPTH):
                body(layer)

        @block.vector
        def _(dve):
            steps = [0]

            def split_lo(layer, u):
                dve.wait_ge(hi_done.sem, hi_done.at(layer, u + 1))
                dve.tensor_tensor(unit(w_lo, u), unit(raw, u), unit(w_hi, u).bitcast(F32), ALU.subtract).then_inc(lo_done_dve.sem, 1)

            def drain_x(layer, b):
                for n in range(2):
                    j = 2 * b + n
                    dve.wait_ge(t_filled.sem, t_filled.at(layer, j + 1))
                    if j == 3:
                        dve.wait_ge(h_lo_done.sem, h_lo_done.at(layer, 1))
                    w = preT[:, layer, HALF * n:HALF * (n + 1)][:, :, None].to_broadcast([P, HALF, P])
                    dve.tensor_tensor(pT[:, j % 3, :].rearrange("p (k t) -> p k t", k=HALF),
                                      T[j % 2][:, :].rearrange("p (k t) -> p k t", k=HALF), w, ALU.mult).then_inc(t_drained.sem, 1)
                for n in range(2):
                    j = 2 * b + n
                    dve.wait_ge(h_hi_done.sem, h_hi_done.at(layer, j + 1))
                    part = (slice(None), slice(HALF * n, HALF * (n + 1)), slice(b * P, (b + 1) * P))
                    dve.tensor_tensor(h_lo[part], pT[:, j % 3, :].rearrange("p (k t) -> p k t", k=HALF),
                                      h_hi[part].bitcast(F32), ALU.subtract).then_inc(h_lo_done.sem, 1)

            def body(layer):
                steps[0] = 0

                def mark(ins):
                    steps[0] += 1
                    ins.then_inc(dve_chain.sem, 1)

                def settle():
                    dve.wait_ge(dve_chain.sem, dve_chain.at(layer, steps[0]))

                def link(ins):
                    mark(ins)
                    settle()

                def drain(j, dst, scale=None):
                    dve.wait_ge(t_filled.sem, t_filled.at(layer, j + 1))
                    if scale is None:
                        ins = dve.tensor_copy(dst, T[j % 2][:, 0:dst.free_size()])
                    else:
                        ins = dve.tensor_scalar(dst, T[j % 2][:, :], scale, None, ALU.mult)
                    ins.then_inc(t_drained.sem, 1)

                def drain_pair(j, dst, scale=None):
                    for n in range(2):
                        drain(j + n, dst[:, 2 * n:2 * n + 2, :].rearrange("p f t -> p (f t)"), scale)

                def drain_mix(j, dst_hi, dst_lo, b):
                    dve.wait_ge(t_filled.sem, t_filled.at(layer, j + 1))
                    part = (slice(None), slice(0, HALF), slice(b * P, (b + 1) * P))
                    src = T[j % 2][:, :].rearrange("p (k t) -> p k t", k=HALF)
                    link(dve.tensor_copy(dst_hi[part], src))
                    dve.tensor_tensor(dst_lo[part], src, dst_hi[part].bitcast(F32), ALU.subtract).then_inc(t_drained.sem, 1)

                def index_key():
                    dve.wait_ge(proj_moved.sem, proj_moved.at(layer, place(layer, TAIL, 1) + 1))
                    for b in range(BLOCKS):
                        mark(dve.bn_stats(ik_st[:, 6 * b:6 * b + 6], ikn[:, b, 0:IDX_DIM]))
                    mark(dve.tensor_scalar(iw.rearrange("p (b h) -> p b h", b=BLOCKS), ikn[:, :, IDX_DIM:IDX_DIM + IDX_HEADS],
                                           IDX_HEADS ** -0.5 * IDX_DIM ** -0.5, None, ALU.mult))
                    settle()
                    for b in range(BLOCKS):
                        ins = dve.bn_aggr(ik_mv[:, 2 * b:2 * b + 2], ik_st[:, 6 * b:6 * b + 6])
                        if b == 0:
                            mark(ins)
                    ins.then_inc(ik_var.sem, 1)
                    dve.wait_ge(ik_rstd.sem, ik_rstd.at(layer, 1))
                    k = ik2[:, :, 0, :]
                    for b in range(BLOCKS):
                        mark(dve.tensor_scalar(ik2[:, b, 0, :], ikn[:, b, 0:IDX_DIM], ik_mv[:, 2 * b:2 * b + 1],
                                               ik_r[:, b:b + 1], ALU.subtract, ALU.mult))
                    settle()
                    wide = [P, BLOCKS, IDX_DIM]
                    link(dve.tensor_tensor(k, k, param("ik_w")[:, None, :].to_broadcast(wide), ALU.mult))
                    link(dve.tensor_tensor(k, k, param("ik_b")[:, None, :].to_broadcast(wide), ALU.add))
                    cos = tab[:, 0, :].rearrange("p (b h d) -> p b h d", b=BLOCKS, d=2 * HD)[:, :, 0, :]
                    sin = tab[:, 1, :].rearrange("p (b h d) -> p b h d", b=BLOCKS, d=2 * HD)[:, :, 0, :]
                    c = ik_tmp[:, 0]
                    s = ik_tmp[:, 1]
                    mark(dve.tensor_tensor(c, k[:, :, 0:2 * HD], cos, ALU.mult))
                    mark(dve.tensor_tensor(s[:, :, 0:HD], k[:, :, HD:2 * HD], sin[:, :, 0:HD], ALU.mult))
                    mark(dve.tensor_tensor(s[:, :, HD:2 * HD], k[:, :, 0:HD], sin[:, :, HD:2 * HD], ALU.mult))
                    settle()
                    link(dve.tensor_tensor(k[:, :, 0:2 * HD], c, s, ALU.add))
                    dve.tensor_copy(ik2[:, :, 1, :], k).then_inc(ik_ready.sem, 1)

                def index_sum(j, b, heads):
                    dve.wait_ge(s_freed.sem, s_freed.at(layer, j + 1))
                    n = P * (b + 1)
                    for i, h in enumerate(heads):
                        first = causal[:, P:SEQ] if b == 0 else causal[:, :]
                        ins = dve.scalar_tensor_tensor(out=work[b][:, :], in0=pbuf[:, j % 4, i * n:(i + 1) * n],
                                                       scalar=iw[:, IDX_HEADS * b + h:IDX_HEADS * b + h + 1],
                                                       in1=first if h == 0 else work[b][:, :], op0=ALU.mult, op1=ALU.add)
                        if i < len(heads) - 1:
                            link(ins)
                    ins.then_inc(idx_used.sem, 1)
                    dve.wait_ge(idx_used.sem, idx_used.at(layer, j + 1))

                def choose(b, rounds):
                    for _ in range(rounds):
                        link(dve.max(top8[:, :], work[b][:, :]))
                        link(dve.match_replace(work[b][:, :], top8[:, :], work[b][:, :], TAKEN))

                def mask_unchosen(b):
                    link(dve.tensor_scalar(work[b][:, :], work[b][:, :], TAKEN_ABOVE, NEG, ALU.is_gt, ALU.mult))
                    if b == 0:
                        link(dve.tensor_tensor(work[b][:, :], work[b][:, :], causal[:, P:SEQ], ALU.min))

                def mask_scores(j, b, n_rows, mask):
                    dve.wait_ge(s_filled.sem, s_filled.at(layer, j + 1))
                    if j in (10, 11):
                        dve.wait_ge(t_filled.sem, t_filled.at(layer, T_PD0 + 1))
                    n, r = P * (b + 1), 4 * (j % 4)
                    for i in range(n_rows):
                        ins = dve.tensor_tensor_reduce(pbuf[:, j % 4, i * n:(i + 1) * n], S[j % 2][:, i * n:(i + 1) * n], mask,
                                                       -1.0, -TAKEN, ALU.add, ALU.min, neg_max[:, r + i:r + i + 1])
                    ins.then_inc(s_freed.sem, 1)

                def combine(j, b, n_heads):
                    n, r = P * (b + 1), 4 * (j % 4)
                    dve.wait_ge(exps_done.sem, exps_done.at(layer, j + 2 - S_DIFF0))
                    for at in (r, r + 4):
                        mark(dve.reciprocal(inv[:, at:at + n_heads], sums[:, at:at + n_heads]))
                    settle()
                    link(dve.tensor_scalar(inv[:, r + 4:r + 4 + n_heads], inv[:, r + 4:r + 4 + n_heads], neg_lam, None, ALU.mult))
                    for i in range(n_heads):
                        p1 = pbuf[:, j % 4 + 1, i * n:(i + 1) * n]
                        mark(dve.tensor_scalar(p1, p1, inv[:, r + 4 + i:r + 5 + i], None, ALU.mult))
                    settle()
                    for i in range(n_heads):
                        p0 = pbuf[:, j % 4, i * n:(i + 1) * n]
                        p1 = pbuf[:, j % 4 + 1, i * n:(i + 1) * n]
                        ins = dve.scalar_tensor_tensor(out=p0, in0=p0, scalar=inv[:, r + i:r + i + 1], in1=p1, op0=ALU.mult, op1=ALU.add)
                        if i < n_heads - 1:
                            mark(ins)
                    ins.then_inc(combined.sem, 1)

                def gated(o, scalars):
                    b, mixer = o % 2, o // 2
                    for h in range(HEADS):
                        part = slice(h * E, (h + 1) * E)
                        ins = dve.scalar_tensor_tensor(out=mixn[:, b, part], in0=O[b][:, part], scalar=scalars[h],
                                                       in1=gate[:, b, mixer, part], op0=ALU.mult, op1=ALU.mult)
                    ins.then_inc(mixn_ready.sem, 1)

                def gate_diff(b):
                    dve.wait_ge(ro_ready.sem, ro_ready.at(layer, b + 1))
                    if b == 0:
                        dve.wait_ge(gate_ready.sem, gate_ready.at(layer, 2))
                    gated(b, [ro[:, HEADS * b + h:HEADS * b + h + 1] for h in range(HEADS)])

                def gate_dsa(b):
                    for use in ((12,), (13, 14))[b]:
                        r, n = 4 * (use % 4), 4 if b == 0 else 2
                        mark(dve.reciprocal(inv[:, r:r + n], sums[:, r:r + n]))
                    settle()
                    dve.wait_ge(o_filled.sem, o_filled.at(layer, 3 + b))
                    gated(2 + b, [inv[:, (h if b == 0 else 4 * (1 + h // 2) + h % 2):][:, 0:1] for h in range(HEADS)])

                def weight_y(b):
                    for n in range(2):
                        dve.wait_ge(y_squared.sem, y_squared.at(layer, 2 * b + n + 1))
                        part = slice(n * WIDTH, (n + 1) * WIDTH)
                        ins = dve.tensor_tensor(y_w[:, b, part], Y[b][n][:, :], param("post")[:, part], ALU.mult)
                    ins.then_inc(y_read.sem, 1)

                def residual(b):
                    dve.wait_ge(y_read.sem, y_read.at(layer, b + 1))
                    dve.wait_ge(ry_ready.sem, ry_ready.at(layer, b + 1))
                    for n in range(2):
                        part = slice(n * WIDTH, (n + 1) * WIDTH)
                        dve.scalar_tensor_tensor(out=xres[:, b, part], in0=y_w[:, b, part], scalar=ry[:, b:b + 1],
                                                 in1=xres[:, b, part], op0=ALU.mult, op1=ALU.add).then_inc(x_ready.sem, 1)

                if layer:
                    drain_x(layer, 1)
                split_lo(layer, 4)
                dve.wait_ge(prm_landed.sem, prm_landed.at(layer, 16))
                lam_a, lam_b = pbuf[:, 0, 0:DIFF_QK], pbuf[:, 0, DIFF_QK:2 * DIFF_QK]
                mark(dve.tensor_tensor_reduce(lam_a, param("lq1"), param("lk1"), 1.0, 0.0, ALU.mult, ALU.add, lam_s[:, 0:1]))
                dve.tensor_tensor_reduce(lam_b, param("lq2"), param("lk2"), 1.0, 0.0, ALU.mult, ALU.add, lam_s[:, 1:2]).then_inc(lam_summed.sem, 1)
                split_lo(layer, 5)
                split_lo(layer, 6)
                split_lo(layer, 8)
                split_lo(layer, 9)
                split_lo(layer, 10)
                index_key()
                if layer == 0:
                    dve.wait_ge(causal_ready, 1)
                drain_pair(T_IQ, iqT)
                split_lo(layer, 12)
                drain(T_IK, ikT[:, :])
                split_lo(layer, 13)
                index_sum(0, 0, (0, 2, 4, 6))
                index_sum(1, 0, (1, 3, 5, 7))
                index_sum(2, 1, (0, 2))
                index_sum(3, 1, (1, 3))
                drain_pair(T_DQ, dqT, DIFF_QK ** -0.5)
                split_lo(layer, 14)
                index_sum(4, 1, (4, 6))
                index_sum(5, 1, (5, 7))
                choose(0, 8)
                mask_unchosen(0)
                drain_pair(T_DK, dkT)
                choose(1, 3)
                mask_scores(6, 0, 4, causal[:, P:SEQ])
                mask_scores(7, 0, 4, causal[:, P:SEQ])
                split_lo(layer, 16)
                dve.wait_ge(lam_exped.sem, lam_exped.at(layer, 1))
                link(dve.tensor_tensor(neg_lam, lam_e[:, 1:2], lam_e[:, 0:1], ALU.subtract))
                link(dve.tensor_tensor(neg_lam, neg_lam, param("lam_init"), ALU.subtract))
                combine(6, 0, HEADS)
                mask_scores(8, 1, 2, causal[:, :])
                mask_scores(9, 1, 2, causal[:, :])
                split_lo(layer, 17)
                drain_pair(T_SQ, sqT, E ** -0.5)
                combine(8, 1, 2)
                drain(T_PD0, pT[:, 0, :])
                mask_scores(10, 1, 2, causal[:, :])
                mask_scores(11, 1, 2, causal[:, :])
                choose(1, 2)
                combine(10, 1, 2)
                drain(T_PD1A, pT[:, 1, :])
                choose(1, 3)
                mask_unchosen(1)
                drain_pair(T_SK, skT)
                split_lo(layer, 18)
                drain(T_PD1B, pT[:, 2, :])
                mask_scores(12, 0, 4, work[0][:, :])
                split_lo(layer, 20)
                gate_diff(0)
                split_lo(layer, 21)
                mask_scores(13, 1, 2, work[1][:, :])
                mask_scores(14, 1, 2, work[1][:, :])
                drain_mix(T_MD0, m_hi, m_lo, 0)
                gate_diff(1)
                drain(T_PS0, pT[:, 0, :])
                split_lo(layer, 22)
                drain_mix(T_MD1, m_hi, m_lo, 1)
                drain(T_PS1A, pT[:, 1, :])
                gate_dsa(0)
                drain(T_PS1B, pT[:, 2, :])
                drain_mix(T_MS0, h_hi, h_lo, 0)
                gate_dsa(1)
                weight_y(0)
                residual(0)
                drain_mix(T_MS1, h_hi, h_lo, 1)
                if layer < DEPTH - 1:
                    split_lo(layer + 1, 0)
                    drain_x(layer + 1, 0)
                    split_lo(layer + 1, 1)
                    split_lo(layer + 1, 2)
                weight_y(1)
                residual(1)
                assert steps[0] == DVE_STEPS, steps[0]

            dve.nop().then_inc(out_unit_used.sem, out_unit_used.before)
            dve.nop().then_inc(y_done.sem, y_done.before)
            dve.nop().then_inc(y_read.sem, y_read.before)
            dve.nop().then_inc(t_drained.sem, t_drained.before)
            dve.nop().then_inc(mixn_ready.sem, mixn_ready.before)
            dve.wait_ge(x_landed[0], 16)
            dve.nop().then_inc(x_ready.sem, 2)
            dve.wait_ge(pre_landed, 16)
            drain_x(0, 0)
            dve.wait_ge(first_piece[1], 1)
            dve.tensor_tensor(w_lo[:, 0, 0:FIRST_TILES, :], raw[:, 0, 0:FIRST_TILES, :], w_hi[:, 0, 0:FIRST_TILES, :].bitcast(F32), ALU.subtract)
            dve.wait_ge(hi_done.sem, 1)
            dve.tensor_tensor(w_lo[:, 0, FIRST_TILES:HALF, :], raw[:, 0, FIRST_TILES:HALF, :], w_hi[:, 0, FIRST_TILES:HALF, :].bitcast(F32), ALU.subtract).then_inc(lo_done_dve.sem, 1)
            dve.wait_ge(x_landed[1], 16)
            dve.nop().then_inc(x_ready.sem, 2)
            drain_x(0, 1)
            split_lo(0, 1)
            split_lo(0, 2)
            for layer in range(DEPTH):
                body(layer)

        @block.gpsimd
        def _(pool):
            steps, setup = [0], [0]

            def root_x(layer, b):
                pool.wait_ge(x_squared.sem, x_squared.at(layer, b + 1))
                mean = ep[:, 4 + b:5 + b]
                pool.tensor_scalar(mean, ms_x[:, b:b + 1], 1.0 / D_MODEL, NORM_EPS, ALU.mult, ALU.add).then_inc(mean_ready.sem, 1)
                pool.wait_ge(mean_ready.sem, mean_ready.at(layer, b + 1))
                pool.tensor_tensor(rx[:, b:b + 1], mean, neg_half[:, 0:1], ALU.pow).then_inc(rx_ready.sem, 1)

            def settle_setup(ins):
                setup[0] += 1
                ins.then_inc(pool_setup, 1)
                pool.wait_ge(pool_setup, setup[0])

            def rotary_tables():
                pool.wait_ge(trig_ready, 1)
                for t, heads, half, at in ((0, IDX_HEADS, HD, 0), (2, HEADS, HS, HD)):
                    sin, cos = (trig[:, 4 + i, :].rearrange("p (b f) -> p b f", b=BLOCKS)[:, :, None, at:at + half]
                                .to_broadcast([P, BLOCKS, heads, half]) for i in range(2))
                    c, s = (tab[:, t + i, :].rearrange("p (b h d) -> p b h d", b=BLOCKS, h=heads) for i in range(2))
                    for part in range(2):
                        to = slice(part * half, (part + 1) * half)
                        settle_setup(pool.tensor_copy(c[:, :, :, to], cos))
                        settle_setup(pool.tensor_scalar(s[:, :, :, to], sin, (-1.0, 1.0)[part], None, ALU.mult))

            def rotary_angles():
                turn_parts = (6.28125, 0.0019350051879882812, 3.019916e-07)
                pi, magic = 3.1415925, 1.5 * 2.0 ** 23
                ang, whole, arg, product = trig[:, 0, :], trig[:, 1, :], trig[:, 2:4, :], trig[:, 6, :]
                pool.wait_ge(small_landed, 32)
                settle_setup(pool.tensor_copy(pos_f[:, :], pos_i[:, :]))
                for b in range(BLOCKS):
                    settle_setup(pool.tensor_scalar(ang[:, b * NF:(b + 1) * NF], frq[:, :], pos_f[:, b:b + 1], None, ALU.mult))
                settle_setup(pool.tensor_scalar(whole, ang, 1.0 / (2.0 * np.pi), magic, ALU.mult, ALU.add))
                settle_setup(pool.tensor_scalar(whole, whole, -magic, None, ALU.add))
                for part in turn_parts:
                    settle_setup(pool.tensor_scalar(product, whole, -part, None, ALU.mult))
                    settle_setup(pool.tensor_tensor(ang, ang, product, ALU.add))
                settle_setup(pool.tensor_copy(arg[:, 0, :], ang))
                settle_setup(pool.tensor_scalar(arg[:, 1, :], ang, 0.5 * np.pi, None, ALU.add))
                settle_setup(pool.tensor_scalar(whole, arg[:, 1, :], pi, -2.0 * np.pi, ALU.is_gt, ALU.mult))
                settle_setup(pool.tensor_tensor(arg[:, 1, :], arg[:, 1, :], whole, ALU.add))
                pool.tensor_scalar(arg, arg, pi, -pi, ALU.min, ALU.max).then_inc(angles_ready, 1)

            def body(layer):
                steps[0] = 0

                def link(ins):
                    steps[0] += 1
                    ins.then_inc(pool_chain.sem, 1)
                    pool.wait_ge(pool_chain.sem, pool_chain.at(layer, steps[0]))

                def inverse_root(dst, src, tmp, scale, eps, signal):
                    link(pool.tensor_scalar(tmp, src, scale, eps, ALU.mult, ALU.add))
                    pool.tensor_tensor(dst, tmp, neg_half[:, 0:dst.free_size()], ALU.pow).then_inc(signal.sem, 1)

                def split_lo(u):
                    pool.wait_ge(hi_done.sem, hi_done.at(layer, u + 1))
                    pool.tensor_tensor(unit(w_lo, u), unit(raw, u), unit(w_hi, u).bitcast(F32), ALU.subtract).then_inc(lo_done_pool.sem, 1)

                def rope(chunk, heads, half, table):
                    pool.wait_ge(proj_moved.sem, proj_moved.at(layer, place(layer, chunk, 1) + 1))
                    order = (IQ, DQ, DK, SQ, SK).index(chunk)
                    slot = order % 2
                    if order:
                        pool.wait_ge(rope_done.sem, rope_done.at(layer, order))
                    v = nat[:, slot, :, :].rearrange("p b (h d) -> p (b h) d", h=heads)
                    cos, sin, c, s = (a.rearrange("p (g d) -> p g d", d=2 * half)
                                      for a in (tab[:, table, :], tab[:, table + 1, :], rt[:, 0, :], rt[:, 1, :]))
                    link(pool.tensor_tensor(c, v[:, :, 0:2 * half], cos, ALU.mult))
                    link(pool.tensor_tensor(s[:, :, 0:half], v[:, :, half:2 * half], sin[:, :, 0:half], ALU.mult))
                    link(pool.tensor_tensor(s[:, :, half:2 * half], v[:, :, 0:half], sin[:, :, half:2 * half], ALU.mult))
                    pool.tensor_tensor(v[:, :, 0:2 * half], c, s, ALU.add).then_inc(rope_done.sem, 1)

                if layer:
                    split_lo(3)
                    root_x(layer, 1)
                else:
                    split_lo(3)
                pool.wait_ge(prm_landed.sem, prm_landed.at(layer, 16))
                link(pool.tensor_scalar(subln, subln, param("one_minus"), None, ALU.mult))
                for b in range(BLOCKS):
                    pool.wait_ge(proj_moved.sem, proj_moved.at(layer, place(layer, DG, b) + 1))
                    g = gate[:, b, 0, :].rearrange("p (h e) -> p h e", h=HEADS)
                    pool.tensor_tensor(g, g, subln[:, None, :].to_broadcast([P, HEADS, E]), ALU.mult).then_inc(gate_ready.sem, 1)
                for g in range(4, GROUPS + 1):
                    if g == 5 and layer == 0:
                        rotary_tables()
                    if g == 6:
                        rope(IQ, IDX_HEADS, HD, 0)
                    if g == 8:
                        pool.wait_ge(ik_var.sem, ik_var.at(layer, 1))
                        link(pool.tensor_scalar(ik_e, ik_mv[:, 1:4:2], LN_EPS, None, ALU.add))
                        pool.tensor_tensor(ik_r, ik_e, neg_half[:, 0:2], ALU.pow).then_inc(ik_rstd.sem, 1)
                    if g == 10:
                        rope(DQ, 2 * HEADS, HD, 0)
                    if g == 12:
                        rope(DK, 2 * HEADS, HD, 0)
                    if g == 14:
                        rope(SQ, HEADS, HS, 2)
                    if g == 16:
                        rope(SK, HEADS, HS, 2)
                    if g in (18, 19):
                        b = g - 18
                        pool.wait_ge(o_squared.sem, o_squared.at(layer, b + 1))
                        part = slice(HEADS * b, HEADS * (b + 1))
                        inverse_root(ro[:, part], ms_o[:, part], ep[:, 8 + 4 * b:12 + 4 * b], 1.0 / E, SUBLN_EPS, ro_ready)
                    if (g + 3) % RING == 3:
                        split_lo(g + 3)
                for b in range(BLOCKS):
                    part, mean = ep[:, 2 * b:2 * b + 1], ep[:, 6 + b:7 + b]
                    pool.wait_ge(y_squared.sem, y_squared.at(layer, 2 * b + 1))
                    link(pool.tensor_scalar(part, part, 1.0 / D_MODEL, NORM_EPS, ALU.mult, ALU.add))
                    pool.wait_ge(y_squared.sem, y_squared.at(layer, 2 * b + 2))
                    link(pool.tensor_scalar(mean, ep[:, 2 * b + 1:2 * b + 2], 1.0 / D_MODEL, part, ALU.mult, ALU.add))
                    pool.tensor_tensor(ry[:, b:b + 1], mean, neg_half[:, 0:1], ALU.pow).then_inc(ry_ready.sem, 1)
                    if b == 0 and layer < DEPTH - 1:
                        root_x(layer + 1, 0)
                assert steps[0] == POOL_STEPS, steps[0]

            settle_setup(pool.memset(ident[:, :], 0.0))
            pool.affine_select(out=ident[:, :], in_=ident[:, :], compare_op=ALU.not_equal, fill=1.0,
                               base=0, pattern=[[-1, P]], channel_multiplier=1).then_inc(ident_ready, 1)
            pool.memset(neg_half, -0.5).then_inc(neg_half_ready, 1)
            settle_setup(pool.memset(causal[:, :], 0.0))
            pool.affine_select(out=causal[:, P:SEQ], in_=causal[:, P:SEQ], compare_op=ALU.is_ge, fill=NEG,
                               base=0, pattern=[[-1, P]], channel_multiplier=1).then_inc(causal_ready, 1)
            rotary_angles()
            root_x(0, 0)
            root_x(0, 1)
            for layer in range(DEPTH):
                body(layer)


DVE_STEPS = 89
POOL_STEPS = 23


def kernel(x, positions, pre_norm_w, post_norm_w, w_in, w_out, lambda_q1, lambda_k1, lambda_q2, lambda_k2,
           diff_subln_w, idx_k_norm_w, idx_k_norm_b):
    import math

    import concourse.bacc as bacc
    from concourse.bass_utils import run_bass_kernel_spmd

    freqs = np.concatenate([np.float32(ROPE_THETA) ** (-np.arange(0, 2 * n, 2, dtype=np.float32) / np.float32(2 * n))
                            for n in (HD, HS)]).astype(np.float32)[None, :]
    init = [0.8 - 0.6 * math.exp(-0.3 * layer) for layer in range(DEPTH)]
    consts = np.array([[v, 1.0 - v] for v in init], np.float32)
    f = np.ascontiguousarray
    arrays = {
        "x": f(x), "positions": f(np.asarray(positions).reshape(BLOCKS, P).T), "freqs": freqs,
        "pre_t": f(np.asarray(pre_norm_w).reshape(DEPTH * KT, P).T),
        "rows": f(np.concatenate([np.asarray(a) for a in (lambda_q1, lambda_k1, lambda_q2, lambda_k2, diff_subln_w,
                                                          idx_k_norm_w, idx_k_norm_b, post_norm_w)] + [consts], axis=1)),
        "w_in": f(w_in), "w_out": f(w_out),
    }
    nc = bacc.Bacc("TRN2", target_bir_lowering=False, num_devices=1)
    args = [nc.dram_tensor(f"in_{name}", a.shape, mybir.dt.from_np(a.dtype), kind="ExternalInput").ap() for name, a in arrays.items()]
    result = nc.dram_tensor("out", (1, SEQ, D_MODEL), F32, kind="ExternalOutput").ap()
    build_trunk(nc, *args, result)
    r = run_bass_kernel_spmd(nc, [{f"in_{name}": a for name, a in arrays.items()}], core_ids=[0])
    return r.results[0]["out"]
```
